# Optimizing a Trainium2 kernel written in Bass

```python
import math
import jax, jax.numpy as jnp
from jax import lax
import numpy as np

D_MODEL = 1024
BATCH = 1
SEQ = 256
DEPTH = 2

PLE_DIM = 256
D_FF = 2816
D_RNN = D_MODEL
RNN_BLOCKS = 16
RNN_BW = D_RNN // RNN_BLOCKS
CONV_W = 4
RG_C = 8.0
N_HEADS = 8
HEAD_DIM = 128
D_ATTN = N_HEADS * HEAD_DIM
Q_BLOCK = 128
N_IN = 2 * D_RNN + 3 * D_ATTN + N_HEADS + 2 * D_MODEL
EPS = 1e-6


def rms_norm(x, g):
    xf = x.astype(jnp.float32)
    y = xf * lax.rsqrt(jnp.mean(xf * xf, axis=-1, keepdims=True) + EPS)
    return (y * g.astype(jnp.float32)).astype(x.dtype)

def swiglu_ffn(h, w_in, w_out):
    g, u = jnp.split(h @ w_in, 2, axis=-1)
    return (jax.nn.silu(g) * u) @ w_out

def causal_dwconv(x, w, b):
    S = x.shape[1]
    xp = jnp.pad(x, ((0, 0), (CONV_W - 1, 0), (0, 0)))
    y = b + xp[:, 0:S] * w[0]
    for k in range(1, CONV_W):
        y = y + xp[:, k:k + S] * w[k]
    return y

def rg_lru(x, w_a, b_a, w_x, b_x, lam):
    B, S, C = x.shape
    xb = x.reshape(B, S, RNN_BLOCKS, RNN_BW)
    r = jax.nn.sigmoid(jnp.einsum('bsnc,ncd->bsnd', xb, w_a).reshape(B, S, C) + b_a)
    i = jax.nn.sigmoid(jnp.einsum('bsnc,ncd->bsnd', xb, w_x).reshape(B, S, C) + b_x)
    log_a = -RG_C * r.astype(jnp.float32) * jax.nn.softplus(-lam.astype(jnp.float32))
    a = jnp.exp(log_a)
    mult = jnp.sqrt(-jnp.expm1(2.0 * log_a))
    u = mult * (i * x).astype(jnp.float32)

    def combine(left, right):
        a1, b1 = left
        a2, b2 = right
        return a1 * a2, a2 * b1 + b2

    _, h = lax.associative_scan(combine, (a, u), axis=1)
    return h.astype(x.dtype)

def forgetting_attention(q, k, v, f_logit, f_b, q_g, k_g):
    B, S, _ = q.shape
    q = rms_norm(q.reshape(B, S, N_HEADS, HEAD_DIM), q_g)
    k = rms_norm(k.reshape(B, S, N_HEADS, HEAD_DIM), k_g)
    v = v.reshape(B, S, N_HEADS, HEAD_DIM)
    log_f = jax.nn.log_sigmoid((f_logit + f_b).astype(jnp.float32))
    dcum = jnp.cumsum(log_f, axis=1).transpose(0, 2, 1)
    qh = q.transpose(0, 2, 1, 3)
    kh = k.transpose(0, 2, 1, 3)
    vh = v.transpose(0, 2, 1, 3)
    nb = S // Q_BLOCK
    q_blocks = qh.reshape(B, N_HEADS, nb, Q_BLOCK, HEAD_DIM).transpose(2, 0, 1, 3, 4)
    d_blocks = dcum.reshape(B, N_HEADS, nb, Q_BLOCK).transpose(2, 0, 1, 3)
    kpos = jnp.arange(S)
    scale = 1.0 / math.sqrt(HEAD_DIM)

    def one_block(args):
        qb, dqb, blk = args
        s = jnp.einsum('bhqd,bhkd->bhqk', qb, kh).astype(jnp.float32) * scale
        s = s + dqb[..., None] - dcum[:, :, None, :]
        qpos = blk * Q_BLOCK + jnp.arange(Q_BLOCK)
        s = jnp.where(kpos[None, :] <= qpos[:, None], s, -jnp.inf)
        pr = jax.nn.softmax(s, axis=-1).astype(vh.dtype)
        return jnp.einsum('bhqk,bhkd->bhqd', pr, vh)

    o = lax.map(one_block, (q_blocks, d_blocks, jnp.arange(nb)))
    return o.transpose(1, 0, 3, 2, 4).reshape(B, S, D_ATTN)

def first_inputs(seed: int = 0) -> dict:
    key = jax.random.key(seed)
    ks = jax.random.split(key, 32)
    f32 = jnp.float32

    def nrm(k, shape, fan_in):
        return jax.random.normal(k, shape, f32) * (fan_in ** -0.5)

    def gain(k, shape):
        return 1.0 + 0.05 * jax.random.normal(k, shape, f32)

    def small(k, shape):
        return 0.02 * jax.random.normal(k, shape, f32)

    a_c = jax.random.uniform(ks[12], (DEPTH, D_RNN), f32, 0.9, 0.999)
    s = a_c ** (1.0 / RG_C)
    rg_lambda = jnp.log(s) - jnp.log1p(-s)

    return {
        "x": jax.random.normal(ks[0], (BATCH, SEQ, D_MODEL), f32),
        "p": jax.random.normal(ks[1], (DEPTH, BATCH, SEQ, PLE_DIM), f32),
        "ffn1_norm": gain(ks[2], (DEPTH, D_MODEL)),
        "ffn1_w_in": nrm(ks[3], (DEPTH, D_MODEL, 2 * D_FF), D_MODEL),
        "ffn1_w_out": nrm(ks[4], (DEPTH, D_FF, D_MODEL), D_FF),
        "mix_norm": gain(ks[5], (DEPTH, D_MODEL)),
        "w_in": nrm(ks[6], (DEPTH, D_MODEL, N_IN), D_MODEL),
        "merge_b": small(ks[7], (DEPTH, 2 * D_MODEL)),
        "conv_w": nrm(ks[8], (DEPTH, CONV_W, D_RNN), CONV_W),
        "conv_b": small(ks[9], (DEPTH, D_RNN)),
        "rg_wa": nrm(ks[10], (DEPTH, RNN_BLOCKS, RNN_BW, RNN_BW), RNN_BW),
        "rg_ba": small(ks[11], (DEPTH, D_RNN)),
        "rg_wx": nrm(ks[13], (DEPTH, RNN_BLOCKS, RNN_BW, RNN_BW), RNN_BW),
        "rg_bx": small(ks[14], (DEPTH, D_RNN)),
        "rg_lambda": rg_lambda,
        "f_b": jax.random.uniform(ks[15], (DEPTH, N_HEADS), f32, 1.0, 4.0),
        "q_norm": gain(ks[16], (DEPTH, HEAD_DIM)),
        "k_norm": gain(ks[17], (DEPTH, HEAD_DIM)),
        "w_rnn_out": nrm(ks[18], (DEPTH, D_RNN, D_MODEL), D_RNN),
        "w_attn_out": nrm(ks[19], (DEPTH, D_ATTN, D_MODEL), D_ATTN),
        "w_o": nrm(ks[20], (DEPTH, D_MODEL, D_MODEL), D_MODEL),
        "ffn2_norm": gain(ks[21], (DEPTH, D_MODEL)),
        "ffn2_w_in": nrm(ks[22], (DEPTH, D_MODEL, 2 * D_FF), D_MODEL),
        "ffn2_w_out": nrm(ks[23], (DEPTH, D_FF, D_MODEL), D_FF),
        "ple_norm": gain(ks[24], (DEPTH, D_MODEL)),
        "ple_w_gate": nrm(ks[25], (DEPTH, D_MODEL, D_MODEL), D_MODEL),
        "ple_b_gate": small(ks[26], (DEPTH, D_MODEL)),
        "ple_w_proj": nrm(ks[27], (DEPTH, PLE_DIM, D_MODEL), PLE_DIM),
        "final_norm": gain(ks[28], (D_MODEL,)),
    }

def first_block(x, p, ffn1_norm, ffn1_w_in, ffn1_w_out, mix_norm, w_in, merge_b,
              conv_w, conv_b, rg_wa, rg_ba, rg_wx, rg_bx, rg_lambda, f_b, q_norm, k_norm,
              w_rnn_out, w_attn_out, w_o, ffn2_norm, ffn2_w_in, ffn2_w_out,
              ple_norm, ple_w_gate, ple_b_gate, ple_w_proj, final_norm):
    split_idx = list(np.cumsum([D_RNN, D_RNN, D_ATTN, D_ATTN, D_ATTN, N_HEADS, D_MODEL]))
    for i in range(DEPTH):
        x = x + 0.5 * swiglu_ffn(rms_norm(x, ffn1_norm[i]), ffn1_w_in[i], ffn1_w_out[i])

        h = rms_norm(x, mix_norm[i])
        proj = h @ w_in[i]
        rx, rgate, q, k, v, f_logit, ga, gb = jnp.split(proj, split_idx, axis=-1)

        rx = causal_dwconv(rx, conv_w[i], conv_b[i])
        ya = rg_lru(rx, rg_wa[i], rg_ba[i], rg_wx[i], rg_bx[i], rg_lambda[i])
        ya = (ya * jax.nn.gelu(rgate)) @ w_rnn_out[i]

        yb = forgetting_attention(q, k, v, f_logit, f_b[i], q_norm[i], k_norm[i]) @ w_attn_out[i]

        mb_a, mb_b = jnp.split(merge_b[i], 2)
        merged = jax.nn.sigmoid(ga + mb_a) * ya + jax.nn.sigmoid(gb + mb_b) * yb
        x = x + merged @ w_o[i]

        x = x + 0.5 * swiglu_ffn(rms_norm(x, ffn2_norm[i]), ffn2_w_in[i], ffn2_w_out[i])

        gate = jax.nn.sigmoid(rms_norm(x, ple_norm[i]) @ ple_w_gate[i] + ple_b_gate[i])
        x = x + gate * (p[i] @ ple_w_proj[i])
    return rms_norm(x, final_norm)


GRID_W = 64
CTX_LEN = 256
A_HEADS = 4
A_KV_HEADS = 2
B_HEADS = 4
B_KV_HEADS = 2
Q_WIDTH = (A_HEADS + B_HEADS) * HEAD_DIM
KV_WIDTH = 2 * (A_KV_HEADS + B_KV_HEADS) * HEAD_DIM
BLOCK = 128
WINDOW = 128
ROPE_THETA = 10000.0
FNET_GROUPS = 4
CONV_W_2 = 3
N_MOD = 6
N_ATTN_LAYERS = (DEPTH + 1) // 2
N_FOURIER_LAYERS = DEPTH // 2


F32 = jnp.float32

def rms_norm_2(x, g):
    xf = x.astype(F32)
    y = xf * lax.rsqrt(jnp.mean(xf * xf, axis=-1, keepdims=True) + EPS)
    return (y * g.astype(F32)).astype(x.dtype)

def modulate(h, shift, scale):
    return h * (1 + scale) + shift

def adaln_params(cond, w, bias):
    m = jax.nn.silu(cond) @ w + bias
    return jnp.split(m[..., None, :], N_MOD, axis=-1)

def axial_rope_tables(row, col):
    n_freq = HEAD_DIM // 4
    inv = ROPE_THETA ** (-jnp.arange(n_freq, dtype=F32) / n_freq)
    ang = jnp.stack([row.astype(F32)[:, None] * inv, col.astype(F32)[:, None] * inv], axis=1)
    return jnp.cos(ang), jnp.sin(ang)

def apply_rope(x, cos, sin):
    b, l, h, dh = x.shape
    xs = x.reshape(b, l, h, 2, 2, dh // 4)
    x1, x2 = xs[..., 0, :], xs[..., 1, :]
    cs = cos[None, :, None].astype(x.dtype)
    sn = sin[None, :, None].astype(x.dtype)
    out = jnp.stack([x1 * cs - x2 * sn, x2 * cs + x1 * sn], axis=-2)
    return out.reshape(b, l, h, dh)

def group_heads(q, n_kv):
    b, l, h, dh = q.shape
    return q.reshape(b, l, n_kv, h // n_kv, dh)

def split_kv(kv):
    b, l, _ = kv.shape
    a = A_KV_HEADS * HEAD_DIM
    bb = B_KV_HEADS * HEAD_DIM
    k_a, v_a, k_b, v_b = jnp.split(kv, [a, 2 * a, 2 * a + bb], axis=-1)
    return (k_a.reshape(b, l, A_KV_HEADS, HEAD_DIM), v_a.reshape(b, l, A_KV_HEADS, HEAD_DIM),
            k_b.reshape(b, l, B_KV_HEADS, HEAD_DIM), v_b.reshape(b, l, B_KV_HEADS, HEAD_DIM))

def attend(q, k, v, sink=None):
    s = jnp.einsum('bqkgd,bskd->bkgqs', q, k, preferred_element_type=F32) * (HEAD_DIM ** -0.5)
    if sink is not None:
        s_sink = jnp.broadcast_to(sink.astype(F32)[None, :, :, None, None], s.shape[:-1] + (1,))
        p = jax.nn.softmax(jnp.concatenate([s_sink, s], axis=-1), axis=-1)[..., 1:]
    else:
        p = jax.nn.softmax(s, axis=-1)
    return jnp.einsum('bkgqs,bskd->bqkgd', p.astype(v.dtype), v)

def global_attention(q, k, v, k_ctx, v_ctx):
    b, l, hkv, g, dh = q.shape
    k_all = jnp.concatenate([k_ctx, k], axis=1)
    v_all = jnp.concatenate([v_ctx, v], axis=1)
    qb = jnp.moveaxis(q.reshape(b, l // BLOCK, BLOCK, hkv, g, dh), 1, 0)
    o = lax.map(lambda qblk: attend(qblk, k_all, v_all), qb)
    return jnp.moveaxis(o, 0, 1).reshape(b, l, hkv * g * dh)

def window_attention(q, k, v, k_ctx, v_ctx, sink):
    b, l, hkv, g, dh = q.shape
    nb = l // BLOCK
    zpad = jnp.zeros((b, BLOCK, hkv, dh), k.dtype)

    def band(t):
        tp = jnp.concatenate([zpad, t, zpad], axis=1).reshape(b, nb + 2, BLOCK, hkv, dh)
        return jnp.concatenate([tp[:, :-2], tp[:, 1:-1], tp[:, 2:]], axis=2)

    kb, vb = band(k), band(v)
    qb = q.reshape(b, nb, BLOCK, hkv, g, dh)
    scale = HEAD_DIM ** -0.5
    s_loc = jnp.einsum('bnqkgd,bnskd->bnkgqs', qb, kb, preferred_element_type=F32) * scale
    s_ctx = jnp.einsum('bnqkgd,bskd->bnkgqs', qb, k_ctx, preferred_element_type=F32) * scale
    qi = jnp.arange(BLOCK)[:, None]
    si = jnp.arange(3 * BLOCK)[None, :]
    in_window = jnp.abs(si - BLOCK - qi) <= WINDOW
    kpos = (jnp.arange(nb)[:, None] - 1) * BLOCK + jnp.arange(3 * BLOCK)[None, :]
    in_range = (kpos >= 0) & (kpos < l)
    valid = in_window[None] & in_range[:, None, :]
    s_loc = jnp.where(valid[None, :, None, None], s_loc, -jnp.inf)
    s_sink = jnp.broadcast_to(sink.astype(F32)[None, None, :, :, None, None], s_ctx.shape[:-1] + (1,))
    p = jax.nn.softmax(jnp.concatenate([s_sink, s_ctx, s_loc], axis=-1), axis=-1)
    c_len = k_ctx.shape[1]
    p_ctx = p[..., 1:1 + c_len].astype(v.dtype)
    p_loc = p[..., 1 + c_len:].astype(v.dtype)
    o = (jnp.einsum('bnkgqs,bskd->bnqkgd', p_ctx, v_ctx)
         + jnp.einsum('bnkgqs,bnskd->bnqkgd', p_loc, vb))
    return o.reshape(b, l, hkv * g * dh)

def attention_mixers(h, hc, w_in, w_out, q_g, k_g, sink, cos, sin, with_ctx_queries):
    b, l, _ = h.shape
    c_len = hc.shape[1]
    proj = h @ w_in
    q_all, kv = proj[..., :Q_WIDTH], proj[..., Q_WIDTH:]
    q_a = q_all[..., :A_HEADS * HEAD_DIM].reshape(b, l, A_HEADS, HEAD_DIM)
    q_b = q_all[..., A_HEADS * HEAD_DIM:].reshape(b, l, B_HEADS, HEAD_DIM)
    k_a, v_a, k_b, v_b = split_kv(kv)
    q_a = apply_rope(rms_norm_2(q_a, q_g), cos, sin)
    k_a = apply_rope(rms_norm_2(k_a, k_g), cos, sin)
    q_b = apply_rope(q_b, cos, sin)
    k_b = apply_rope(k_b, cos, sin)
    k_ac, v_ac, k_bc, v_bc = split_kv(hc @ w_in[:, Q_WIDTH:])
    k_ac = rms_norm_2(k_ac, k_g)
    sink_hg = sink.reshape(B_KV_HEADS, B_HEADS // B_KV_HEADS)
    o_a = global_attention(group_heads(q_a, A_KV_HEADS), k_a, v_a, k_ac, v_ac)
    o_b = window_attention(group_heads(q_b, B_KV_HEADS), k_b, v_b, k_bc, v_bc, sink_hg)
    y = jnp.concatenate([o_a, o_b], axis=-1) @ w_out
    if not with_ctx_queries:
        return y, None
    qc = hc @ w_in[:, :Q_WIDTH]
    qc_a = rms_norm_2(qc[..., :A_HEADS * HEAD_DIM].reshape(b, c_len, A_HEADS, HEAD_DIM), q_g)
    qc_b = qc[..., A_HEADS * HEAD_DIM:].reshape(b, c_len, B_HEADS, HEAD_DIM)
    oc_a = attend(group_heads(qc_a, A_KV_HEADS), k_ac, v_ac).reshape(b, c_len, -1)
    oc_b = attend(group_heads(qc_b, B_KV_HEADS), k_bc, v_bc, sink_hg).reshape(b, c_len, -1)
    yc = jnp.concatenate([oc_a, oc_b], axis=-1) @ w_out
    return y, yc

def fourier_mix(h):
    b, l, d = h.shape
    hg = h.reshape(b, l, FNET_GROUPS, d // FNET_GROUPS).astype(F32)
    f = jnp.fft.fft2(hg, axes=(1, 3), norm="ortho").real
    return f.reshape(b, l, d).astype(h.dtype)

def conv_ffn(h, w_up, conv_w, conv_b, w_down):
    u = h @ w_up
    up = jnp.pad(u, ((0, 0), (1, 1), (0, 0)))
    u = up[:, :-2] * conv_w[0] + up[:, 1:-1] * conv_w[1] + up[:, 2:] * conv_w[2] + conv_b
    gate, val = jnp.split(u, 2, axis=-1)
    return (jax.nn.silu(gate) * val) @ w_down

def second_inputs(seed: int = 0) -> dict:
    key = jax.random.key(seed)
    ks = jax.random.split(key, 17)

    def nrm(k, shape, scale):
        return jax.random.normal(k, shape, F32) * scale

    return {
        "x": nrm(ks[0], (BATCH, SEQ, D_MODEL), 1.0),
        "c": nrm(ks[1], (BATCH, D_MODEL), 1.0),
        "ctx": nrm(ks[2], (BATCH, CTX_LEN, D_MODEL), 1.0),
        "c_ctx": nrm(ks[3], (D_MODEL,), 1.0),
        "mod_w": nrm(ks[4], (DEPTH, D_MODEL, N_MOD * D_MODEL), 0.5 * D_MODEL ** -0.5),
        "mod_b": nrm(ks[5], (DEPTH, N_MOD * D_MODEL), 0.02),
        "norm_g": 1.0 + nrm(ks[6], (DEPTH, 4, D_MODEL), 0.02),
        "attn_w_in": nrm(ks[7], (N_ATTN_LAYERS, D_MODEL, Q_WIDTH + KV_WIDTH), D_MODEL ** -0.5),
        "attn_w_out": nrm(ks[8], (N_ATTN_LAYERS, Q_WIDTH, D_MODEL), Q_WIDTH ** -0.5),
        "q_norm_g": 1.0 + nrm(ks[9], (N_ATTN_LAYERS, HEAD_DIM), 0.02),
        "k_norm_g": 1.0 + nrm(ks[10], (N_ATTN_LAYERS, HEAD_DIM), 0.02),
        "sink": nrm(ks[11], (N_ATTN_LAYERS, B_HEADS), 0.5),
        "fourier_w_out": nrm(ks[12], (N_FOURIER_LAYERS, D_MODEL, D_MODEL), D_MODEL ** -0.5),
        "ffn_w_up": nrm(ks[13], (DEPTH, D_MODEL, 2 * D_FF), D_MODEL ** -0.5),
        "ffn_conv_w": nrm(ks[14], (DEPTH, CONV_W_2, 2 * D_FF), CONV_W_2 ** -0.5),
        "ffn_conv_b": nrm(ks[15], (DEPTH, 2 * D_FF), 0.02),
        "ffn_w_down": nrm(ks[16], (DEPTH, D_FF, D_MODEL), D_FF ** -0.5),
    }

def second_block(x, c, ctx, c_ctx, mod_w, mod_b, norm_g, attn_w_in, attn_w_out, q_norm_g, k_norm_g, sink,
              fourier_w_out, ffn_w_up, ffn_conv_w, ffn_conv_b, ffn_w_down):
    b, l, d = x.shape
    rows = l // GRID_W
    row = jnp.repeat(jnp.arange(rows), GRID_W)
    col = jnp.tile(jnp.arange(GRID_W), rows)
    cos, sin = axial_rope_tables(row, col)

    for i in range(DEPTH):
        ctx_next = any(j % 2 == 0 for j in range(i + 1, DEPTH))
        need_hc = (i % 2 == 0) or ctx_next
        sh1, sc1, g1, sh2, sc2, g2 = adaln_params(c, mod_w[i], mod_b[i])
        h = modulate(rms_norm_2(x, norm_g[i, 0]), sh1, sc1)
        if need_hc:
            csh1, csc1, cg1, csh2, csc2, cg2 = adaln_params(c_ctx, mod_w[i], mod_b[i])
            hc = modulate(rms_norm_2(ctx, norm_g[i, 0]), csh1, csc1)
        if i % 2 == 0:
            a = i // 2
            y, yc = attention_mixers(h, hc, attn_w_in[a], attn_w_out[a], q_norm_g[a], k_norm_g[a], sink[a],
                                     cos, sin, ctx_next)
        else:
            w_f = fourier_w_out[i // 2]
            y = fourier_mix(h) @ w_f
            yc = fourier_mix(hc) @ w_f if ctx_next else None
        x = x + g1 * rms_norm_2(y, norm_g[i, 1])
        h = modulate(rms_norm_2(x, norm_g[i, 2]), sh2, sc2)
        x = x + g2 * rms_norm_2(conv_ffn(h, ffn_w_up[i], ffn_conv_w[i], ffn_conv_b[i], ffn_w_down[i]), norm_g[i, 3])
        if ctx_next:
            ctx = ctx + cg1 * rms_norm_2(yc, norm_g[i, 1])
            hc = modulate(rms_norm_2(ctx, norm_g[i, 2]), csh2, csc2)
            ctx = ctx + cg2 * rms_norm_2(conv_ffn(hc, ffn_w_up[i], ffn_conv_w[i], ffn_conv_b[i], ffn_w_down[i]),
                                       norm_g[i, 3])
    return x


def setup_inputs(seed=0):
    out = dict(first_inputs(seed))
    for name, value in second_inputs(seed + 1).items():
        if name != "x":
            out[name + "_2"] = value
    return out


def reference(
    x, p, ffn1_norm, ffn1_w_in, ffn1_w_out, mix_norm, w_in, merge_b, conv_w, conv_b, rg_wa,
    rg_ba, rg_wx, rg_bx, rg_lambda, f_b, q_norm, k_norm, w_rnn_out, w_attn_out, w_o, ffn2_norm,
    ffn2_w_in, ffn2_w_out, ple_norm, ple_w_gate, ple_b_gate, ple_w_proj, final_norm, c_2, ctx_2,
    c_ctx_2, mod_w_2, mod_b_2, norm_g_2, attn_w_in_2, attn_w_out_2, q_norm_g_2, k_norm_g_2,
    sink_2, fourier_w_out_2, ffn_w_up_2, ffn_conv_w_2, ffn_conv_b_2, ffn_w_down_2,
):
    x = first_block(
        x, p, ffn1_norm, ffn1_w_in, ffn1_w_out, mix_norm, w_in, merge_b, conv_w, conv_b, rg_wa,
        rg_ba, rg_wx, rg_bx, rg_lambda, f_b, q_norm, k_norm, w_rnn_out, w_attn_out, w_o,
        ffn2_norm, ffn2_w_in, ffn2_w_out, ple_norm, ple_w_gate, ple_b_gate, ple_w_proj,
        final_norm,
    )
    return second_block(
        x, c_2, ctx_2, c_ctx_2, mod_w_2, mod_b_2, norm_g_2, attn_w_in_2, attn_w_out_2,
        q_norm_g_2, k_norm_g_2, sink_2, fourier_w_out_2, ffn_w_up_2, ffn_conv_w_2, ffn_conv_b_2,
        ffn_w_down_2,
    )


_drawn_inputs = setup_inputs


def setup_inputs(seed=0):
    import zlib

    import numpy as np

    out = dict(_drawn_inputs(seed))
    spreads = {}
    factors = {'merge_b': 8.0,
     'rg_ba': 8.0,
     'rg_bx': 8.0,
     'q_norm': 6.101,
     'k_norm': 6.807,
     'ple_norm': 4.831,
     'ple_b_gate': 8.0,
     'norm_g_2': 3.253,
     'q_norm_g_2': 8.0,
     'k_norm_g_2': 8.0,
     'sink_2': 64.0,
     'ffn_conv_b_2': 5.802}
    for name, (base, spread) in spreads.items():
        noise = np.random.default_rng([zlib.crc32(name.encode()), seed]).standard_normal(out[name].shape)
        drawn = base * np.exp(spread * noise) if base else spread * noise
        out[name] = __import__('jax').numpy.asarray(drawn.astype(out[name].dtype))
    for name, factor in factors.items():
        out[name] = (out[name] * factor).astype(out[name].dtype)
    return out
```

```python
from contextlib import ExitStack, contextmanager

import numpy as np

import concourse.bass as bass
from concourse import mybir

P = 128
F32 = mybir.dt.float32
F32R = mybir.dt.float32r
ALU = mybir.AluOpType
ACT = mybir.ActivationFunctionType
AX = mybir.AxisListType.X

S = 256
ST = S // P
D = 1024
KD = D // P
F = 2816
KF = F // P
L = 2
NH = 8
HD = 128
PLE = 256
KP = PLE // P
EPS = 1e-6
SCALE = HD ** -0.5
RG_C = 8.0
NEG = -3.0e38
CONV = 4
RNN_BW = 64
MODS = 6
NKV2 = 4
NG = 4
GD = D // NG
GRID_W = 64
WINDOW = 128
MOD_UNIT = 512
MOD_TURNS = L * MODS * D // MOD_UNIT // (2 * L)
CTX_TURNS = 2 * D // MOD_UNIT // (2 * L)
UNIT_TURNS = MOD_TURNS + CTX_TURNS
UNIT_CHUNKS = MOD_UNIT // P
MODCOL = L * MODS * KD

SLOTS = 4
LEAD = 3
TMAX = KF // 2
RX, RGATE, QC, KC, VC, GA, GB, NPROJ = 0, 8, 16, 24, 32, 40, 48, 56


def column_map():
    at, n = {}, 0
    for name, k in (("ffn1_norm", L * KD), ("mix_norm", L * KD), ("ffn2_norm", L * KD), ("ple_norm", L * KD),
                    ("merge_b", L * 2 * KD), ("conv_w", L * CONV * KD), ("conv_b", L * KD), ("rg_ba", L * KD),
                    ("rg_bx", L * KD), ("rg_lambda", L * KD), ("q_norm", L), ("k_norm", L), ("ple_b_gate", L * KD),
                    ("final_norm", KD), ("c_2", KD), ("c_ctx_2", KD), ("mod_b_2", L * MODS * KD),
                    ("norm_g_2", L * 4 * KD), ("q_norm_g_2", 1), ("k_norm_g_2", 1),
                    ("ffn_conv_w_2", L * 3 * 2 * KF), ("ffn_conv_b_2", L * 2 * KF)):
        at[name] = n
        n += k
    return at, n


COL, NCOL = column_map()

TABS = {"ident": (0, P), "causal": (P, P)}
TABS2 = {"swap": (0, P), "cos": (P, S), "sin": (P + S, S), "window": (P + 2 * S, ST * S)}
NTAB, NTAB2 = 2 * P, P + (2 + ST) * S

SEGS = []
for _l in range(L):
    SEGS += [("ffn1_in", 2 * KF, KD, _l * 2 * KF), ("ffn1_out", 2 * KD, KF // 2, _l * 2 * KD),
             ("mix_in", NPROJ, KD, _l * NPROJ), ("rnn_out", KD, KD, _l * KD), ("attn_out", KD, KD, _l * KD),
             ("mix_out", KD, KD, _l * KD), ("ffn2_in", 2 * KF, KD, _l * 2 * KF),
             ("ffn2_out", 2 * KD, KF // 2, _l * 2 * KD), ("ple", KD, KD + KP, _l * KD)]
SEGS += [("attn2_in", 2 * KD, KD, 0), ("attn2_out", KD, KD, 0), ("ffn3_in", 2 * KF, KD, 0),
         ("ffn3_out", 2 * KD, KF // 2, 0), ("fourier_out", KD, KD, 0), ("ffn3_in", 2 * KF, KD, 2 * KF),
         ("ffn3_out", 2 * KD, KF // 2, 2 * KD)]
BLOCK1 = 9
NSEG = len(SEGS)
X_UPDATES = 5 * KD
HBUF = [sum(_s[0] in ("ffn1_out", "ffn2_out", "ple") for _s in SEGS[:_k]) % 2 for _k in range(NSEG)]


class Semaphores:

    def __init__(self, sem):
        self.hi_done = sem("hi_done")
        self.lo_done = sem("lo_done")
        self.mm_done = sem("mm_done")
        self.evicted = sem("evicted")
        self.x_ready = sem("x_ready")
        self.h_hi = sem("h_hi")
        self.rhs_ready = sem("rhs_ready")
        self.sq_ready = sem("sq_ready")
        self.ssq_add = sem("ssq_add")
        self.ssq_mm = sem("ssq_mm")
        self.rms_ready = sem("rms_ready")
        self.hn_ready = sem("hn_ready")
        self.in_consts = sem("in_consts")
        self.in_x = sem("in_x")
        self.in_ctx = sem("in_ctx")
        self.in_p = sem("in_p")
        self.in_rnn = sem("in_rnn")
        self.in_dft = sem("in_dft")
        self.consts = sem("consts")
        self.lam_exp = sem("lam_exp")
        self.wf_hi = sem("wf_hi")
        self.wf_ready = sem("wf_ready")
        self.silu_done = sem("silu_done")
        self.prod_ready = sem("prod_ready")
        self.act_hi = sem("act_hi")
        self.act_ready = sem("act_ready")
        self.conv_mid = sem("conv_mid")
        self.f_mm = sem("f_mm")
        self.f_z = sem("f_z")
        self.f_exp = sem("f_exp")
        self.dcum_ready = sem("dcum_ready")
        self.ws_ready = sem("ws_ready")
        self.conv_first = sem("conv_first")
        self.xc_ready = sem("xc_ready")
        self.gates_mm = sem("gates_mm")
        self.ri_done = sem("ri_done")
        self.at_done = sem("at_done")
        self.m_ready = sem("m_ready")
        self.mult_done = sem("mult_done")
        self.u_ready = sem("u_ready")
        self.scan_done = sem("scan_done")
        self.gelu_done = sem("gelu_done")
        self.gated = sem("gated")
        self.gated_hi = sem("gated_hi")
        self.gated_ready = sem("gated_ready")
        self.sig_done = sem("sig_done")
        self.qk_sq = sem("qk_sq")
        self.qk_ssq = sem("qk_ssq")
        self.qk_rms = sem("qk_rms")
        self.qk_normed = sem("qk_normed")
        self.staged = sem("staged")
        self.v_mm = sem("v_mm")
        self.vt_ready = sem("vt_ready")
        self.dsel_ready = sem("dsel_ready")
        self.s_mm = sem("s_mm")
        self.max_ready = sem("max_ready")
        self.exp_done = sem("exp_done")
        self.p_ready = sem("p_ready")
        self.pt_mm = sem("pt_mm")
        self.ptc_ready = sem("ptc_ready")
        self.o_mm = sem("o_mm")
        self.o_hi = sem("o_hi")
        self.o_ready = sem("o_ready")
        self.rot_mm = sem("rot_mm")
        self.rope_part = sem("rope_part")
        self.roped = sem("roped")
        self.y_gated = sem("y_gated")
        self.merged = sem("merged")
        self.merged_hi = sem("merged_hi")
        self.merged_ready = sem("merged_ready")
        self.pt_hi = sem("pt_hi")
        self.pt_ready = sem("pt_ready")
        self.gate_in = sem("gate_in")
        self.gate_sig = sem("gate_sig")
        self.silu_c = sem("silu_c")
        self.ptd_ready = sem("ptd_ready")
        self.spec_half = sem("spec_half")
        self.hf_raw = sem("hf_raw")
        self.hf_ready = sem("hf_ready")
        self.unit_scaled = sem("unit_scaled")
        self.unit_sum = sem("unit_sum")
        self.unit_acc = sem("unit_acc")
        self.mods_in = sem("mods_in")
        self.unit_mm = sem("unit_mm")
        self.mods_ready = sem("mods_ready")
        self.spec_mm = sem("spec_mm")
        self.spec_ready = sem("spec_ready")
        self.four_mm = sem("four_mm")
        self.dve_chain = sem("dve_chain")
        self.act_chain = sem("act_chain")
        self.pool_chain = sem("pool_chain")
        self.stored = sem("stored")


class Tally:

    def __init__(self, start=0):
        self.n, self.turn, self.per = start, None, 0

    def at(self, off=0):
        return self.n + off if self.turn is None else self.turn * self.per + (self.n + off)

    def take(self, k=1, off=0):
        self.n += k
        return self.at(off)


@contextmanager
def rolled(eng, start, end, tallies, per):
    n0 = [t.n for t in tallies]
    with eng.Fori(start, end) as i:
        for t, k in zip(tallies, per):
            t.n, t.turn, t.per = (t.n - start * k, i, k) if k else (t.n, None, 0)
        n1 = [t.n for t in tallies]
        yield i
        assert [t.n - a for t, a in zip(tallies, n1)] == list(per)
    for t, a, k in zip(tallies, n0, per):
        t.n, t.turn, t.per = a + (end - start) * k, None, 0


MAIN, CTX = 0, KD


def unit_turns(eng, n, tallies, extra, per_extra, body, last=None, first=1):
    before = [t.n for t in tallies]
    body(0, None)
    per = [t.n - a for t, a in zip(tallies, before)]
    for i in range(1, first):
        body(i, None)
    c, x = first + MOD_TURNS, first + UNIT_TURNS
    for start, end, unit in ((first, c, MAIN), (c, x, CTX), (x, n - 1 if last else n, None)):
        if end == start + 1:
            body(start, unit)
        else:
            with rolled(eng, start, end, tallies + extra, per + (list(per_extra) if unit is not None else [0] * len(extra))) as i:
                body(i, unit)
    if last:
        last(n - 1)


def turns(eng, n, tallies, body, last=None):
    before = [t.n for t in tallies]
    body(0)
    per = [t.n - a for t, a in zip(tallies, before)]
    end = n - 1 if last else n
    if end > 2:
        with rolled(eng, 1, end, tallies, per) as i:
            body(i)
    elif end == 2:
        body(1)
    if last:
        last(n - 1)


def wait(eng, semaphore, value):
    if not isinstance(value, int) or value > 0:
        eng.wait_ge(semaphore, value)


def build_program(nc, d, out):
    with ExitStack() as ctx:
        def sb(name, shape, dt=F32):
            return ctx.enter_context(nc.sbuf_tensor(name, shape, dt))

        def sem(name):
            return ctx.enter_context(nc.semaphore(name))

        def area(name, nbytes):
            start = (nc.sbuf_base + 31) // 32 * 32
            sb(name, [P, nbytes // 4])
            used = [0]

            def place(tname, shape, dt=F32, at=None):
                size = 4 * int(np.prod(shape[1:]))
                off = used[0] if at is None else at
                assert off + size <= nbytes, (tname, off, size, nbytes)
                used[0] = off + size
                return nc.alloc_sbuf_tensor_at(tname, shape, dt, offset=start + off)
            return place

        raw = [sb(f"raw{i}", [P, TMAX * P]) for i in range(SLOTS)]
        whi = [sb(f"whi{i}", [P, TMAX * P], F32R) for i in range(SLOTS)]
        wlo = [sb(f"wlo{i}", [P, TMAX * P], F32R) for i in range(SLOTS)]
        x = sb("x", [P, KD, S])
        hspace = area("hspace", 4 * KD * S * 4)
        hhi = [hspace(f"hhi{i}", [P, KD, S], F32R) for i in range(2)]
        hlo = [hspace(f"hlo{i}", [P, KD, S], F32R) for i in range(2)]
        unit = [[hspace(f"unit{i}{half}", [P, KD // 2, MOD_UNIT], at=(i + 2 * half) * KD * S * 4) for half in range(2)]
                for i in range(2)]
        cols = sb("cols", [P, NCOL, 1])
        tabs = sb("tabs", [P, NTAB])
        rms = sb("rms", [P, S])
        rstd = sb("rstd", [P, S])
        sq = sb("sq", [P, 2, S])
        ssq = sb("ssq", [P, S])
        ones = sb("ones", [P, S])
        neg_ones = sb("neg_ones", [P, P])
        eps_col = sb("eps_col", [P, 1])
        modv = sb("modv", [P, MODCOL + 2 * KD, 1])
        gmod = sb("gmod", [P, (4 * L + 1) * KD, 1])
        neg_sp = sb("neg_sp", [P, L * KD, 1])
        pos_sp = sb("pos_sp", [P, L * KD, 1])
        gq = sb("gq", [P, L, 1])
        silu_c = sb("silu_c", [P, 2 * KD, 1])
        FB_COL, SINK_COL, ONEHOT_COL = 0, L, 8
        wf_hi = sb("wf_hi", [P, L * KD * NH], F32R)
        wf_lo = sb("wf_lo", [P, L * KD * NH], F32R)
        small = sb("small", [P, 16, 1])
        stat = [sb(f"stat{i}", [P, 8]) for i in range(2)]
        big = area("big", NPROJ * S * 4)
        proj = big("proj", [P, NPROJ, S], at=0)
        acthi = big("acthi", [P, KF, S], F32R, at=0)
        actlo = big("actlo", [P, KF, S], F32R)
        kv2 = big("kv2", [P, 2 * NKV2, 2 * S], at=8 * S * 4)
        p2 = [big(f"p2{i}", [P, ST, 2 * S]) for i in range(2)]
        pt2 = [big(f"pt2{i}", [P, 2 * ST, S]) for i in range(2)]
        vt2 = big("vt2", [P, NKV2, 2 * ST, P])
        tabs2 = big("tabs2", [P, NTAB2])
        hf = big("hf", [P, KD, S], at=0)
        dft = big("dft", [P, 2, 2, 2, GD])
        spec = [big(f"spec{i}", [P, ST, 2 * GD]) for i in range(2)]
        wf_raw = big("wf_raw", [P, L * KD * NH], at=0)
        lam_t = [big(f"lam{i}", [P, L * KD]) for i in range(6)]
        inp = big("inp", [P, KD, S], at=20480)
        wide = area("wide", KD * S * 4)
        rnnw = wide("rnnw", [P, KD, 2, P], at=0)
        y = wide("y", [P, KD, S], at=0)
        fstage = area("fstage", 8 * S * 4)
        gr, ur, sg, pr = [[fstage(f"{n}{i}", [P, S]) for i in range(2)] for n in ("gr", "ur", "sg", "pr")]
        ft = [fstage(f"ft{i}", [NH, S], at=i * S * 4) for i in range(8)]
        ptraw = wide("ptraw", [P, KP, S], at=0)
        pthi = wide("pthi", [P, KP, S], F32R)
        ptlo = wide("ptlo", [P, KP, S], F32R)
        mstage = area("mstage", 14 * 1024)
        xc = [mstage(f"xc{i}", [P, S], at=i * 1024) for i in range(2)]
        ri = [mstage(f"ri{i}", [P, 2, S]) for i in range(2)]
        ea = [mstage(f"ea{i}", [P, S]) for i in range(2)]
        th = [mstage(f"th{i}", [P, S]) for i in range(2)]
        u0 = [mstage(f"u0{i}", [P, S]) for i in range(2)]
        mm = ur
        wst = gr
        qs = [mstage(f"qs{i}", [P, S], at=i * 1024) for i in range(2)]
        vs = [mstage(f"vs{i}", [P, S]) for i in range(2)]
        vt = [mstage(f"vt{i}", [P, ST, P]) for i in range(2)]
        pp = [mstage(f"pp{i}", [P, 3 * P]) for i in range(2)]
        ptp = [mstage(f"ptp{i}", [P, 3 * P]) for i in range(2)]
        dsel = [mstage(f"dsel{i}", [NH, S]) for i in range(2)]
        qk2 = mstage("qk2", [P, 2, 2 * S], at=0)
        rqk = mstage("rqk", [P, 2, 2 * S])
        qk2b = [qk2[:, j, :] for j in range(2)]
        rqkb = [rqk[:, j, :] for j in range(2)]
        ra, rb = [[mstage(f"{n}{i}", [P, S]) for i in range(2)] for n in ("ra", "rb")]
        hn = [mstage(f"hn{i}", [P, S], at=i * 1024) for i in range(2)]
        unit_sums = [mstage(f"unit_sum{i}", [P, MOD_UNIT], at=i * MOD_UNIT * 4) for i in range(2)]

        psum = [ctx.enter_context(nc.psum_tensor(f"bank{i}", [P, 512], F32)) for i in range(8)]
        NORM, FB, GEN = psum[4], psum[5], [psum[6], psum[7]]
        SC = [psum[4], psum[5]]

        landed = [sem(f"landed{i}") for i in range(SLOTS)]
        in_unit = [sem(f"in_unit{i}") for i in range(2)]
        q = Semaphores(sem)

        def col(name, k=0):
            return cols[:, COL[name] + k, :]

        def tab(name):
            table, (a, n) = (tabs, TABS[name]) if name in TABS else (tabs2, TABS2[name])
            return table[:, a:a + n]

        ident = tab("ident")

        def f32(ap):
            return ap.bitcast(F32)

        def segment(tallies, eng, k, split, evict, straight=False, units=None, lead=LEAD):
            _, n, tiles, _ = SEGS[k]

            def turn(i, unit=None, final=False):
                for s in range(SLOTS):
                    if not final or s < SLOTS - lead:
                        split((s + lead) % SLOTS, tiles)
                    elif k + 1 < NSEG:
                        split((s + lead) % SLOTS, SEGS[k + 1][2])
                    evict(i, s)
                    if unit is not None:
                        units[0](unit, s)
            if straight:
                for i in range(n // SLOTS):
                    turn(i, final=i == n // SLOTS - 1)
            elif units:
                unit_turns(eng, n // SLOTS, tallies, units[1], units[2], turn, last=lambda i: turn(i, final=True))
            else:
                turns(eng, n // SLOTS, tallies, turn, last=lambda i: turn(i, final=True))

        heads_qk = proj[:, :, :].rearrange("p (g c) s -> p g c s", c=NH)[:, QC // NH:KC // NH + 1]

        K2, V2 = (0, 1, 4, 5), (2, 3, 6, 7)
        NORMED = [(proj[:, 2 * g:2 * g + 2, :], "q_norm_g_2") if kind == 0 else
                  (kv2[:, K2[g], :].rearrange("p (a s) -> p a s", a=2), "k_norm_g_2") for g in range(2) for kind in range(2)]
        ROPED = [proj[:, h, :] for h in range(NH)] + [kv2[:, K2[g], 0:S] for g in range(NKV2)]

        def mod(l, j):
            return (l * MODS + j) * KD

        def gm(l, j):
            return (l * 4 + j) * KD

        def takes_units(k):
            return SEGS[k][0] in ("ffn1_in", "ffn2_in")

        block = ctx.enter_context(nc.Block())

        @block.sync
        def _(sp):
            panel = Tally()
            tallies = [panel]

            def load(name, first, s, i):
                wait(sp, q.lo_done, panel.take(off=-SLOTS))
                tiles = d[name].shape[2] // P
                sp.dma_start(raw[s][:, 0:tiles * P], d[name][SLOTS * i + s + first]).then_inc(landed[s], 16)

            sp.dma_start(cols[:, :, :], d["cols"]).then_inc(q.in_consts, 16)
            sp.dma_start(x[:, :, :], d["x"]).then_inc(q.in_x, 16)
            sp.dma_start(tabs[:, :], d["tabs"]).then_inc(q.in_consts, 16)
            sp.dma_start(wf_raw[:, :], d["w_f"]).then_inc(q.in_consts, 16)
            sp.dma_start(small[:, :, :], d["small"]).then_inc(q.in_consts, 16)

            units_a, units_b = Tally(-1), Tally(-1)

            def load_unit(k, index):
                for j, (used, n) in enumerate(((q.unit_sum, units_b), (q.unit_acc, units_a))):
                    half = 1 - j
                    wait(sp, used, n.take())
                    sp.dma_start(unit[1 - HBUF[k]][half][:, :, :], d["mod_w"][2 * index + half]).then_inc(in_unit[half], 16)

            def beside(k):
                name = SEGS[k][0]
                l = k // BLOCK1
                if name == "mix_in":
                    sp.wait_ge(q.consts, 2 + l)
                    for half in range(2):
                        for kind in range(2):
                            w = slice(half * RNN_BW, (half + 1) * RNN_BW)
                            sp.dma_start(rnnw[w, :, kind, w], d["rnn_gates"][l, kind, half]).then_inc(q.in_rnn, 16)
                if name == "ple":
                    sp.wait_ge(q.gates_mm, KD * (l + 1))
                    sp.dma_start(ptraw[:, :, :], d["p"][l]).then_inc(q.in_p, 16)
                if name == "attn2_in":
                    sp.wait_ge(q.mm_done, sum(s[1] for s in SEGS[:k - 1]))
                    sp.dma_start(inp[:, :, :], d["ctx"]).then_inc(q.in_ctx, 16)
                    sp.dma_start(tabs2[:, :], d["tabs2"]).then_inc(q.in_ctx, 16)
                if name == "fourier_out":
                    sp.wait_ge(q.mm_done, sum(s[1] for s in SEGS[:k]))
                    sp.dma_start(dft[:, :, :, :, :], d["dft"]).then_inc(q.in_dft, 16)

            for k in range(NSEG):
                name, n, tiles, first = SEGS[k]
                for s in range(SLOTS):
                    load(name, first, s, 0)
                beside(k)

                def turn(i, unit_kind=None):
                    for s in range(SLOTS):
                        load(name, first, s, i + 1)
                        if s == 1 and unit_kind == MAIN:
                            load_unit(k, i + (MOD_TURNS * done - 1))
                        elif s == 1 and unit_kind == CTX:
                            load_unit(k, i + (CTX_TURNS * done - MOD_TURNS - 1))
                if takes_units(k):
                    done = sum(takes_units(j) for j in range(k))
                    wait(sp, q.mm_done, sum(s[1] for s in SEGS[:k]))
                    unit_turns(sp, n // SLOTS - 1, tallies, [units_a, units_b], (1, 1), turn)
                else:
                    turns(sp, n // SLOTS - 1, tallies, turn)
            sp.wait_ge(q.x_ready, X_UPDATES)
            sp.dma_start(out, x[:, :, :]).then_inc(q.stored, 16)
            sp.wait_ge(q.stored, 16)

        @block.tensor
        def _(pe):
            panel, act, ssq_n = Tally(), Tally(), Tally()
            h_n, gated_n, o_n, merged_n = Tally(), Tally(), Tally(), Tally()
            tallies = [panel]

            def product(bank, s, t, hi, lo, start, stop):
                w = slice(t * P, (t + 1) * P)
                nc.tensor.matmul(bank, whi[s][:, w], hi, start=start, stop=False)
                nc.tensor.matmul(bank, whi[s][:, w], lo, start=False, stop=False)
                return nc.tensor.matmul(bank, wlo[s][:, w], hi, start=False, stop=stop)

            def ready(s):
                pe.wait_ge(q.lo_done, panel.take())
                wait(pe, q.evicted, panel.at(-SLOTS))

            def norm_sum():
                pe.wait_ge(q.ssq_add, ssq_n.take(KD))
                nc.tensor.matmul(NORM[:, 0:S], ones[:, 0:P], ssq[:, :], start=True, stop=True).then_inc(q.ssq_mm, 1)

            def from_h(k, b, operand, chunks, deferred=False, forget=None, context=None, extra=None):
                _, n, tiles, _ = SEGS[k]

                def turn(i, unit_kind=None):
                    for s in range(SLOTS):
                        ready(s)
                        for t in range(KD):
                            if isinstance(i, int) and i == 0 and s == 0:
                                pe.wait_ge(operand, chunks.take())
                            last = product(psum[s][:, 0:S], s, t, hhi[b][:, t, :], hlo[b][:, t, :], t == 0, t == KD - 1)
                        if extra:
                            if isinstance(i, int) and i == 0 and s == 0:
                                pe.wait_ge(q.pt_ready, extra)
                            for t in range(KP):
                                last = product(psum[s][:, S:2 * S], s, KD + t, pthi[:, t, :], ptlo[:, t, :],
                                               t == 0, t == KP - 1)
                        last.then_inc(q.mm_done, 1)
                        if isinstance(i, int) and i == 0 and s == 1:
                            if deferred:
                                norm_sum()
                            if forget is not None:
                                forget_gates(forget, b)
                        if unit_kind is not None and s == 0:
                            unit_columns(i - 2)
                if takes_units(k):
                    wait(pe, q.mods_in, sum(takes_units(j) for j in range(k)))
                    unit_turns(pe, n // SLOTS, tallies, [acc_n, sum_n], (1, 1), turn, first=2)
                else:
                    turns(pe, n // SLOTS, tallies, turn)

            acc_n, sum_n = Tally(), Tally()

            def unit_columns(u):
                pe.wait_ge(q.unit_acc, acc_n.take())
                pe.wait_ge(q.unit_sum, sum_n.take())
                for c in range(UNIT_CHUNKS):
                    for j in range(2):
                        last = nc.tensor.matmul(GEN[0][:, bass.ds(UNIT_CHUNKS * u + c, 1)], unit_sums[j][:, c * P:(c + 1) * P],
                                                ones[:, 0:1], start=j == 0, stop=j == 1)
                last.then_inc(q.unit_mm, 1)

            def forget_gates(l, b):
                if l == 0:
                    pe.wait_ge(q.wf_ready, 1)
                for t in range(KD):
                    w = slice((l * KD + t) * NH, (l * KD + t + 1) * NH)
                    nc.tensor.matmul(FB[0:NH, 0:S], wf_hi[:, w], hhi[b][:, t, :], start=t == 0, stop=False)
                    nc.tensor.matmul(FB[0:NH, 0:S], wf_hi[:, w], hlo[b][:, t, :], start=False, stop=False)
                    last = nc.tensor.matmul(FB[0:NH, 0:S], wf_lo[:, w], hhi[b][:, t, :], start=False, stop=t == KD - 1)
                last.then_inc(q.f_mm, 1)

            def from_act(k):
                def turn(i):
                    for s in range(SLOTS):
                        ready(s)
                        half = s % 2
                        bank = psum[s - half][:, 0:S]
                        for t in range(TMAX):
                            c = half * TMAX + t
                            if isinstance(i, int) and i == 0 and s < 2:
                                pe.wait_ge(q.act_ready, act.take())
                            last = product(bank, s, t, acthi[:, c, :], actlo[:, c, :], c == 0, c == KF - 1)
                        last.then_inc(q.mm_done, 1)
                turns(pe, SEGS[k][1] // SLOTS, tallies, turn)

            ws_n, xc_n, ri_n = Tally(), Tally(), Tally(-2)
            rnn_tallies = [ws_n, xc_n, ri_n]

            def rnn_gates():
                def turn(i):
                    for j in range(2):
                        pe.wait_ge(q.ws_ready, ws_n.take())
                        pe.wait_ge(q.xc_ready, xc_n.take())
                        wait(pe, q.ri_done, ri_n.take())
                        nc.tensor.matmul(GEN[j][:, 0:S], wst[j][:, 0:P], xc[j][:, :], start=True, stop=True)
                        nc.tensor.matmul(GEN[j][:, S:2 * S], wst[j][:, P:2 * P], xc[j][:, :],
                                         start=True, stop=True).then_inc(q.gates_mm, 1)
                turns(pe, KD // 2, rnn_tallies, turn)

            qsq_n, qrms_n, st_n, vt_n, ds_n, exp_n, p_n, ptc_n, oe_n = (
                Tally(), Tally(-2), Tally(), Tally(), Tally(), Tally(-2), Tally(), Tally(), Tally(-2))
            att_tallies = [qsq_n, qrms_n, st_n, vt_n, ds_n, exp_n, p_n, ptc_n, oe_n]

            def attention():
                def norms(i):
                    for j in range(2):
                        pe.wait_ge(q.qk_sq, qsq_n.take())
                        wait(pe, q.qk_rms, qrms_n.take())
                        nc.tensor.matmul(GEN[j][:, :], ones[:, 0:P], qk2b[j], start=True, stop=True).then_inc(q.qk_ssq, 1)
                turns(pe, NH // 2, att_tallies, norms)
                pe.wait_ge(q.qk_normed, qk_normed_n.take(NH))

                def heads(i):
                    for j in range(2):
                        h = 2 * i + j
                        pe.wait_ge(q.staged, st_n.take())
                        wait(pe, q.o_ready, oe_n.take())
                        for t in range(ST):
                            last = nc.tensor.transpose(GEN[j][:, t * P:(t + 1) * P], vs[j][:, t * P:(t + 1) * P], ident)
                        last.then_inc(q.v_mm, 1)
                        pe.wait_ge(q.dsel_ready, ds_n.take())
                        wait(pe, q.exp_done, exp_n.take())
                        sc = SC[j]
                        for t in range(ST):
                            o, n = t * P, (t + 1) * P
                            dst = sc[:, o:o + n]
                            nc.tensor.matmul(dst, qs[j][:, t * P:(t + 1) * P], proj[:, KC + h, 0:n], start=True, stop=False)
                            nc.tensor.matmul(dst, dsel[j][:, t * P:(t + 1) * P], ones[0:NH, 0:n], start=False, stop=False)
                            nc.tensor.matmul(dst, neg_ones[0:NH, :], dsel[j][:, 0:n], start=False, stop=False)
                            last = nc.tensor.matmul(sc[:, o + t * P:o + n], ident, tab("causal"), start=False, stop=True)
                        last.then_inc(q.s_mm, 1)
                    for j in range(2):
                        pe.wait_ge(q.p_ready, p_n.take())
                        pe.wait_ge(q.vt_ready, vt_n.take())
                        for dst, src in ((0, 0), (1, 1), (2, 2)):
                            last = nc.tensor.transpose(GEN[j][:, dst * P:(dst + 1) * P], pp[j][:, src * P:(src + 1) * P], ident)
                        last.then_inc(q.pt_mm, 1)
                    for j in range(2):
                        pe.wait_ge(q.ptc_ready, ptc_n.take())
                        nc.tensor.matmul(GEN[j][:, 0:S], vt[j][:, 0, :], ptp[j][:, 0:S], start=True, stop=False,
                                         skip_group_check=True)
                        nc.tensor.matmul(GEN[j][:, P:S], vt[j][:, 1, :], ptp[j][:, S:3 * P], start=False, stop=True,
                                         skip_group_check=True).then_inc(q.o_mm, 1)
                turns(pe, NH // 2, att_tallies, heads)
            qk_normed_n = Tally()

            def attn2_in(k, b):
                for i in range(SEGS[k][1]):
                    s = i % SLOTS
                    ready(s)
                    for t in range(KD):
                        if i == 0:
                            pe.wait_ge(q.rhs_ready, h_n.take())
                        last = product(psum[s][:, 0:S], s, t, hhi[b][:, t, :], hlo[b][:, t, :], t == 0, t == KD - 1)
                    for t in range(KD if i >= KD else 0):
                        if i == KD:
                            pe.wait_ge(q.rhs_ready, h_n.take())
                        last = product(psum[s][:, S:2 * S], s, t, hhi[1 - b][:, t, :], hlo[1 - b][:, t, :], t == 0, t == KD - 1)
                    last.then_inc(q.mm_done, 1)

            def attention2():
                pe.wait_ge(q.evicted, panel.at())
                pe.wait_ge(q.in_ctx, 32)
                for n, _ in enumerate(NORMED):
                    pe.wait_ge(q.qk_sq, qsq_n.take())
                    wait(pe, q.qk_rms, qrms_n.take())
                    nc.tensor.matmul(GEN[n % 2][:, :], ones[:, 0:P], qk2b[n % 2], start=True, stop=True).then_inc(q.qk_ssq, 1)
                pe.wait_ge(q.qk_normed, qk_normed_n.take(len(NORMED)))
                for n, item in enumerate(ROPED):
                    if n >= 2:
                        pe.wait_ge(q.rope_part, n - 1)
                    nc.tensor.matmul(GEN[n % 2][:, 0:S], tab("swap"), item, start=True, stop=True).then_inc(q.rot_mm, 1)
                for g in range(NKV2):
                    pe.wait_ge(q.rope_part, len(ROPED) - 1 + g) if g < 2 else pe.wait_ge(q.vt_ready, L * NH + g - 1)
                    for t in range(2 * ST):
                        last = nc.tensor.transpose(GEN[g % 2][:, t * P:(t + 1) * P], kv2[:, V2[g], t * P:(t + 1) * P], ident)
                    last.then_inc(q.v_mm, 1)
                pe.wait_ge(q.roped, len(ROPED))

                def scores(h):
                    g, j = h // 2, h % 2
                    if h >= 2:
                        pe.wait_ge(q.exp_done, L * NH + h - 1)
                    for t in range(ST):
                        windowed = g >= NKV2 // 2
                        last = nc.tensor.matmul(psum[2 * j + t][:, :], proj[:, h, t * P:(t + 1) * P], kv2[:, K2[g], :],
                                                start=True, stop=not windowed)
                        if windowed:
                            last = nc.tensor.matmul(psum[2 * j + t][:, 0:S], ident, tab("window")[:, t * S:(t + 1) * S],
                                                    start=False, stop=True)
                    last.then_inc(q.s_mm, 1)

                def weigh(h):
                    g, j = h // 2, h % 2
                    pe.wait_ge(q.p_ready, L * NH + h + 1)
                    if h >= 1:
                        pe.wait_ge(q.ptc_ready, L * NH + h)
                        pe.wait_ge(q.ptd_ready, h)
                    for kt in range(2 * ST):
                        for t in range(ST):
                            o = (kt % 2) * S + t * P
                            last = nc.tensor.transpose(psum[4 + kt // 2][:, o:o + P], p2[j][:, t, kt * P:(kt + 1) * P], ident)
                    last.then_inc(q.pt_mm, 1)
                    pe.wait_ge(q.ptc_ready, L * NH + h + 1)
                    pe.wait_ge(q.ptd_ready, h + 1)
                    if h == 0:
                        pe.wait_ge(q.vt_ready, L * NH + NKV2)
                    if h >= 2:
                        pe.wait_ge(q.o_ready, L * NH + h - 1)
                    for kt in range(2 * ST):
                        last = nc.tensor.matmul(GEN[j][:, 0:S], vt2[:, g, kt, :], pt2[j][:, kt, :],
                                                start=kt == 0, stop=kt == 2 * ST - 1)
                    last.then_inc(q.o_mm, 1)
                for h in range(NH + 1):
                    if h < NH:
                        scores(h)
                    if h >= 1:
                        weigh(h - 1)

            def fourier():
                pe.wait_ge(q.in_dft, 16)

                def spectrum(g):
                    if g >= 2:
                        pe.wait_ge(q.spec_half, g - 1)
                        pe.wait_ge(q.spec_ready, g - 1)
                    for t in range(ST):
                        for r in range(2):
                            if t == 0:
                                pe.wait_ge(q.hf_ready, 2 * g + r + 1)
                            last = nc.tensor.matmul(psum[2 * (g % 2) + t][:, :], hf[:, 2 * g + r, t * P:(t + 1) * P],
                                                    dft[:, 0, r, :, :], start=r == 0, stop=r == 1)
                    last.then_inc(q.spec_mm, 1)

                def along_tokens(g):
                    pe.wait_ge(q.spec_half, g + 1)
                    pe.wait_ge(q.spec_ready, g + 1)
                    for r in range(2):
                        if g >= 1:
                            pe.wait_ge(q.rhs_ready, h_n.at() + 2 * (g - 1) + r + 1)
                        for t in range(ST):
                            for cs in range(2):
                                o = cs * GD + r * P
                                last = nc.tensor.matmul(GEN[r][:, 0:S], spec[g % 2][:, t, o:o + P], dft[:, 1, t, cs, :],
                                                        start=t + cs == 0, stop=t + cs == 2)
                        last.then_inc(q.four_mm, 1)
                for g in range(NG + 1):
                    if g < NG:
                        spectrum(g)
                    if g >= 1:
                        along_tokens(g - 1)

            pe.wait_ge(q.consts, 1)
            b = 0
            for k in range(NSEG):
                name = SEGS[k][0]
                l = k // BLOCK1
                if name in ("ffn1_in", "ffn2_in"):
                    from_h(k, b, q.rhs_ready, h_n, deferred=True)
                elif name in ("ffn1_out", "ffn2_out"):
                    from_act(k)
                    b = 1 - b
                elif name == "mix_in":
                    from_h(k, b, q.rhs_ready, h_n, deferred=True, forget=l)
                    pe.wait_ge(q.mods_in, sum(takes_units(j) for j in range(k)))
                    rnn_gates()
                    attention()
                elif name == "rnn_out":
                    from_h(k, 1 - b, q.gated_ready, gated_n)
                elif name == "attn_out":
                    from_h(k, b, q.o_ready, o_n)
                elif name == "mix_out":
                    from_h(k, 1 - b, q.merged_ready, merged_n)
                elif name == "ple":
                    from_h(k, b, q.rhs_ready, h_n, deferred=True, extra=l + 1)
                    b = 1 - b
                elif name == "attn2_in":
                    norm_sum()
                    norm_sum()
                    norm_sum()
                    attn2_in(k, b)
                    attention2()
                elif name == "attn2_out":
                    from_h(k, b, q.o_ready, o_n)
                    norm_sum()
                    norm_sum()
                elif name == "ffn3_in":
                    from_h(k, b, q.rhs_ready, h_n)
                elif name == "ffn3_out":
                    from_act(k)
                    norm_sum()
                    if k + 1 < NSEG:
                        norm_sum()
                        fourier()
                elif name == "fourier_out":
                    from_h(k, b, q.rhs_ready, h_n)
                    norm_sum()
                    norm_sum()

        @block.scalar
        def _(act):
            ahead, seen, prod_n, x_n, sq_free = Tally(), Tally(), Tally(), Tally(), Tally(-2)
            land = [Tally() for _ in range(SLOTS)]
            merged_n, gate_n, chain = Tally(), Tally(), Tally()
            tallies = [ahead, seen, prod_n, sq_free, merged_n, gate_n] + land

            def split(s, tiles):
                act.wait_ge(landed[s], land[s].take(16))
                wait(act, q.mm_done, ahead.take(off=-SLOTS))
                nc.scalar.activation(whi[s][:, 0:tiles * P], raw[s][:, 0:tiles * P], ACT.Copy).then_inc(q.hi_done, 1)

            def link(ins):
                ins.then_inc(q.act_chain, 1)
                act.wait_ge(q.act_chain, chain.take())

            ssq_n = Tally()

            def norm_rstd():
                act.wait_ge(q.ssq_mm, ssq_n.take())
                link(nc.scalar.activation(rms[:, :], NORM[:, 0:S], ACT.Ln, bias=eps_col[:, :], scale=1.0 / D))
                nc.scalar.activation(rstd[:, :], rms[:, :], ACT.Exp, scale=-0.5).then_inc(q.rms_ready, 1)

            def next_operand(c, parity, gain, buf):
                wait(act, q.ssq_add, sq_free.take())
                if gain is not None:
                    nc.scalar.activation(hhi[buf][:, c, :], x[:, c, :], ACT.Copy, scale=gain(c)).then_inc(q.h_hi, 1)
                nc.scalar.activation(sq[:, parity, :], x[:, c, :], ACT.Square).then_inc(q.sq_ready, 1)

            def gain_of(name, l):
                return lambda c: cols[:, COL[name] + l * KD + c, :]

            def ffn_in(k, root=True):
                def evict(i, s):
                    if root and isinstance(i, int) and i == 0 and s == 0:
                        norm_rstd()
                    j = s // 2
                    if s % 2 == 0:
                        act.wait_ge(q.evicted, seen.take())
                        nc.scalar.activation(sg[j][:, :], gr[j][:, :], ACT.Silu).then_inc(q.silu_done, 1)
                    else:
                        seen.take()
                        act.wait_ge(q.prod_ready, prod_n.take())
                        nc.scalar.activation(acthi[:, 2 * i + j, :], pr[j][:, :], ACT.Copy).then_inc(q.act_hi, 1)

                def weigh(c0, s):
                    if s == 0:
                        act.wait_ge(in_unit[1], unit_n.take(16))
                        for t in range(KD // 2):
                            u = unit[1 - HBUF[k]][1][:, t, :]
                            last = nc.scalar.activation(u, u, ACT.Copy, scale=silu_c[:, c0 + KD // 2 + t, :])
                        last.then_inc(q.unit_scaled, 1)
                segment(tallies, act, k, split, evict, lead=SLOTS, units=(weigh, [unit_n], (16,)))

            unit_n = Tally()

            def ffn_out(k, gain, buf):
                def evict(i, s):
                    if s % 2:
                        if isinstance(i, int) and i == 0 and s == 1:
                            act.wait_ge(q.unit_mm, UNIT_TURNS * sum(takes_units(j) for j in range(k)))
                        act.wait_ge(q.evicted, seen.take(2))
                        next_operand(2 * i + s // 2, s // 2, gain, buf)
                segment(tallies, act, k, split, evict, lead=SLOTS)

            def into_x(k, gain, buf, gated=None):
                def evict(i, s):
                    c = SLOTS * i + s
                    if gated is not None:
                        if isinstance(i, int) and i == 0 and s == 0:
                            norm_rstd()
                        act.wait_ge(q.gate_in, gate_n.take())
                        nc.scalar.activation(sg[s % 2][:, :], gr[s % 2][:, :], ACT.Sigmoid,
                                             bias=cols[:, gated + c, :]).then_inc(q.gate_sig, 1)
                    act.wait_ge(q.evicted, seen.take())
                    next_operand(c, s % 2, gain, buf)
                segment(tallies, act, k, split, evict, lead=SLOTS)

            def mix_in(k):
                def evict(i, s):
                    if isinstance(i, int) and i == 0 and s == 0:
                        norm_rstd()
                    seen.take()
                segment(tallies, act, k, split, evict, lead=SLOTS)

            def plain(k):
                def evict(i, s):
                    seen.take()
                segment(tallies, act, k, split, evict, lead=SLOTS)

            def attn_out(k, buf):
                def evict(i, s):
                    seen.take()
                    act.wait_ge(q.merged, merged_n.take())
                    c = SLOTS * i + s
                    nc.scalar.activation(hhi[buf][:, c, :], proj[:, GA + c, :], ACT.Copy).then_inc(q.merged_hi, 1)
                segment(tallies, act, k, split, evict, lead=SLOTS)

            fz_n = Tally()

            def forget_gates():
                act.wait_ge(q.f_z, fz_n.take())
                link(nc.scalar.activation(ft[1][:, :], ft[0][:, :], ACT.Abs))
                nc.scalar.activation(ft[1][:, :], ft[1][:, :], ACT.Exp, scale=-1.0).then_inc(q.f_exp, 1)

            u_n, conv_n, g_n, r_n, m_n, sc_n = Tally(-2), Tally(), Tally(), Tally(), Tally(), Tally(-2)
            gl_n = Tally()

            def recurrence(l, buf):
                def turn(i):
                    for j in range(2):
                        c = 2 * i + j
                        wait(act, q.u_ready, u_n.take())
                        nc.scalar.activation(xc[j][:, :], proj[:, RX + c, :], ACT.Identity,
                                             bias=cols[:, COL["conv_b"] + l * KD + c, :],
                                             scale=cols[:, COL["conv_w"] + (l * CONV + CONV - 1) * KD + c, :]
                                             ).then_inc(q.conv_first, 1)
                    for j in range(2):
                        c = 2 * i + j
                        act.wait_ge(q.gates_mm, g_n.take())
                        for kind, name in enumerate(("rg_ba", "rg_bx")):
                            last = nc.scalar.activation(ri[j][:, kind, :], GEN[j][:, kind * S:(kind + 1) * S], ACT.Sigmoid,
                                                        bias=cols[:, COL[name] + l * KD + c, :])
                        last.then_inc(q.ri_done, 1)
                    for j in range(2):
                        c = 2 * i + j
                        act.wait_ge(q.ri_done, r_n.take())
                        wait(act, q.scan_done, sc_n.take())
                        nc.scalar.activation(ea[j][:, :], ri[j][:, 0, :], ACT.Exp, scale=neg_sp[:, l * KD + c, :])
                        nc.scalar.activation(th[j][:, :], ri[j][:, 0, :], ACT.Tanh,
                                             scale=pos_sp[:, l * KD + c, :]).then_inc(q.at_done, 1)
                    for j in range(2):
                        act.wait_ge(q.m_ready, m_n.take())
                        nc.scalar.activation(mm[j][:, :], mm[j][:, :], ACT.Sqrt).then_inc(q.mult_done, 1)
                turns(act, KD // 2, [u_n, g_n, r_n, m_n, sc_n], turn)

                def gelu(i):
                    for j in range(2):
                        c = 2 * i + j
                        nc.scalar.activation(proj[:, RGATE + c, :], proj[:, RGATE + c, :], ACT.Gelu_apprx_tanh
                                             ).then_inc(q.gelu_done, 1)
                    for j in range(2):
                        c = 2 * i + j
                        act.wait_ge(q.gated, gl_n.take())
                        nc.scalar.activation(hhi[buf][:, c, :], proj[:, RX + c, :], ACT.Copy).then_inc(q.gated_hi, 1)
                turns(act, KD // 2, [gl_n], gelu)

            qs_n, qn_n = Tally(), Tally(-2)
            v_n, om_free, mx_n, pt_n, o_n = Tally(), Tally(-2), Tally(), Tally(), Tally()

            def attention(buf):
                def norms(i):
                    for j in range(2):
                        h = 2 * i + j
                        nc.scalar.activation(qk2b[j].rearrange("p (a s) -> p a s", a=2), heads_qk[:, :, h, :], ACT.Square
                                             ).then_inc(q.qk_sq, 1)
                    for j in range(2):
                        act.wait_ge(q.qk_ssq, qs_n.take())
                        wait(act, q.qk_normed, qn_n.take())
                        link(nc.scalar.activation(rqkb[j], GEN[j][:, :], ACT.Ln, bias=eps_col[:, :], scale=1.0 / HD))
                        nc.scalar.activation(rqkb[j], rqkb[j], ACT.Exp, scale=-0.5).then_inc(q.qk_rms, 1)
                turns(act, NH // 2, [qs_n, qn_n, chain], norms)

                def heads(i):
                    for j in range(2):
                        act.wait_ge(q.v_mm, v_n.take())
                        wait(act, q.o_mm, om_free.take())
                        nc.scalar.activation(vt[j][:, :, :], GEN[j][:, 0:S], ACT.Copy).then_inc(q.vt_ready, 1)
                    for j in range(2):
                        act.wait_ge(q.max_ready, mx_n.take())
                        for t in range(ST):
                            w = slice(t * P, t * P + (t + 1) * P)
                            last = nc.scalar.activation(pp[j][:, w], SC[j][:, w], ACT.Exp, bias=stat[j][:, t:t + 1],
                                                        accum_out=stat[j][:, 2 + t:3 + t])
                        last.then_inc(q.exp_done, 1)
                    for j in range(2):
                        act.wait_ge(q.pt_mm, pt_n.take())
                        nc.scalar.activation(ptp[j][:, :], GEN[j][:, 0:3 * P], ACT.Copy).then_inc(q.ptc_ready, 1)
                    for j in range(2):
                        h = 2 * i + j
                        act.wait_ge(q.o_mm, o_n.take())
                        nc.scalar.activation(hhi[buf][:, h, :], GEN[j][:, 0:S], ACT.Copy).then_inc(q.o_hi, 1)
                turns(act, NH // 2, [v_n, om_free, mx_n, pt_n, o_n], heads)

            def gate_sigmoids(l):
                def turn(i):
                    for s in range(4):
                        n = 4 * i + s
                        nc.scalar.activation(proj[:, GA + n, :], proj[:, GA + n, :], ACT.Sigmoid,
                                             bias=cols[:, COL["merge_b"] + l * 2 * KD + n, :]).then_inc(q.sig_done, 1)
                turns(act, 2 * KD // 4, [], turn)

            xr_n, hn_n = Tally(), Tally()

            def squares_of(source, semaphore, per_chunk):
                def turn(i):
                    for j in range(2):
                        if semaphore is not None:
                            act.wait_ge(semaphore, per_chunk.take())
                        wait(act, q.ssq_add, sq_free.take())
                        nc.scalar.activation(sq[:, j, :], source[:, 2 * i + j, :], ACT.Square).then_inc(q.sq_ready, 1)
                turns(act, KD // 2, [sq_free] + ([per_chunk] if per_chunk else []), turn)

            def shifted(shift, buf):
                def turn(i):
                    for j in range(2):
                        c = 2 * i + j
                        act.wait_ge(q.hn_ready, hn_n.take())
                        nc.scalar.activation(hhi[buf][:, c, :], hn[j][:, :], ACT.Identity, bias=modv[:, shift + c, :]
                                             ).then_inc(q.h_hi, 1)
                turns(act, KD // 2, [hn_n], turn)

            def residual(shift, buf):
                norm_rstd()
                squares_of(x, q.x_ready, xr_n)
                norm_rstd()
                shifted(shift, buf)

            def y_out(k, per):
                def evict(i, s):
                    if per == 1 or s % 2:
                        c = SLOTS * i + s if per == 1 else 2 * i + s // 2
                        act.wait_ge(q.evicted, seen.take(per))
                        wait(act, q.ssq_add, sq_free.take())
                        parity = s % 2 if per == 1 else s // 2
                        nc.scalar.activation(sq[:, parity, :], y[:, c, :], ACT.Square).then_inc(q.sq_ready, 1)
                segment(tallies, act, k, split, evict, lead=SLOTS)

            def ffn_conv_in(k, l):
                def evict(i, s):
                    j = s // 2
                    n = SLOTS * i + s
                    act.wait_ge(q.mm_done, seen.at(1))
                    dst = (gr if s % 2 == 0 else ur)[j]
                    nc.scalar.activation(dst[:, :], psum[s][:, 0:S], ACT.Identity,
                                         scale=cols[:, COL["ffn_conv_w_2"] + (3 * l + 1) * 2 * KF + n, :],
                                         bias=cols[:, COL["ffn_conv_b_2"] + 2 * l * KF + n, :]).then_inc(q.conv_mid, 1)
                    if s % 2 == 0:
                        act.wait_ge(q.evicted, seen.take())
                        nc.scalar.activation(sg[j][:, :], gr[j][:, :], ACT.Silu).then_inc(q.silu_done, 1)
                    else:
                        seen.take()
                        act.wait_ge(q.prod_ready, prod_n.take())
                        nc.scalar.activation(acthi[:, 2 * i + j, :], pr[j][:, :], ACT.Copy).then_inc(q.act_hi, 1)
                segment(tallies, act, k, split, evict, lead=SLOTS)

            def attention2(buf):
                act.wait_ge(q.evicted, seen.at())
                for n, (item, _) in enumerate(NORMED):
                    nc.scalar.activation(qk2[:, n % 2, :].rearrange("p (a s) -> p a s", a=2), item, ACT.Square).then_inc(q.qk_sq, 1)
                    act.wait_ge(q.qk_ssq, qs_n.take())
                    wait(act, q.qk_normed, qn_n.take())
                    link(nc.scalar.activation(rqkb[n % 2], GEN[n % 2][:, :], ACT.Ln, bias=eps_col[:, :], scale=1.0 / HD))
                    nc.scalar.activation(rqkb[n % 2], rqkb[n % 2], ACT.Exp, scale=-0.5).then_inc(q.qk_rms, 1)
                for g in range(NKV2):
                    act.wait_ge(q.v_mm, v_n.take())
                    nc.scalar.activation(vt2[:, g, :, :], GEN[g % 2][:, :], ACT.Copy).then_inc(q.vt_ready, 1)

                def exps(h):
                    j = h % 2
                    act.wait_ge(q.max_ready, mx_n.take())
                    for t in range(ST):
                        if h // 2 >= NKV2 // 2:
                            nc.scalar.activation(stat[j][:, 6 + t:7 + t], small[:, SINK_COL + h - NH // 2, :], ACT.Exp,
                                                 bias=stat[j][:, t:t + 1])
                        last = nc.scalar.activation(p2[j][:, t, :], psum[2 * j + t][:, :], ACT.Exp, bias=stat[j][:, t:t + 1],
                                                    scale=SCALE, accum_out=stat[j][:, 2 + t:3 + t])
                    last.then_inc(q.exp_done, 1)

                def outputs(h):
                    act.wait_ge(q.pt_mm, pt_n.take())
                    nc.scalar.activation(pt2[h % 2][:, 0:2, :], psum[4][:, :], ACT.Copy).then_inc(q.ptc_ready, 1)
                    act.wait_ge(q.o_mm, o_n.take())
                    nc.scalar.activation(hhi[buf][:, h, :], GEN[h % 2][:, 0:S], ACT.Copy).then_inc(q.o_hi, 1)
                for h in range(NH + 1):
                    if h < NH:
                        exps(h)
                    if h >= 1:
                        outputs(h - 1)

            def fourier(shift, buf):
                for c in range(KD):
                    act.wait_ge(q.hf_raw, c + 1)
                    nc.scalar.activation(hf[:, c, :], hf[:, c, :], ACT.Identity, bias=modv[:, shift + c, :]).then_inc(q.hf_ready, 1)
                for g in range(NG + 1):
                    if g < NG:
                        act.wait_ge(q.spec_mm, g + 1)
                        nc.scalar.activation(spec[g % 2][:, 0, :], psum[2 * (g % 2)][:, :], ACT.Copy).then_inc(q.spec_half, 1)
                    for r in range(2 if g >= 1 else 0):
                        c = 2 * (g - 1) + r
                        act.wait_ge(q.four_mm, c + 1)
                        nc.scalar.activation(hhi[buf][:, c, :], GEN[r][:, 0:S], ACT.Copy).then_inc(q.h_hi, 1)

            act.wait_ge(q.in_consts, 64)
            nc.scalar.activation(wf_hi[:, :], wf_raw[:, :], ACT.Copy).then_inc(q.wf_hi, 1)
            lam = cols[:, COL["rg_lambda"]:COL["rg_lambda"] + L * KD, 0]
            link(nc.scalar.activation(lam_t[0][:, :], lam, ACT.Abs))
            nc.scalar.activation(lam_t[0][:, :], lam_t[0][:, :], ACT.Exp, scale=-1.0).then_inc(q.lam_exp, 1)
            act.wait_ge(q.in_x, 16)
            act.wait_ge(q.consts, 1)
            for s in range(SLOTS):
                split(s, SEGS[0][2])
            turns(act, KD // 2, [sq_free], lambda i: [next_operand(2 * i + j, j, gain_of("ffn1_norm", 0), 0) for j in range(2)])

            b = 0
            layer2 = 0
            nc.scalar.activation(silu_c[:, :, 0], cols[:, COL["c_2"]:COL["c_2"] + 2 * KD, 0], ACT.Silu).then_inc(q.silu_c, 1)
            for k in range(NSEG):
                name = SEGS[k][0]
                l = k // BLOCK1
                if name in ("ffn1_in", "ffn2_in"):
                    ffn_in(k)
                elif name == "ffn1_out":
                    ffn_out(k, gain_of("mix_norm", l), 1 - b)
                    b = 1 - b
                elif name == "ffn2_out":
                    ffn_out(k, gain_of("ple_norm", l), 1 - b)
                    b = 1 - b
                elif name == "mix_in":
                    mix_in(k)
                    act.wait_ge(q.evicted, seen.at())
                    forget_gates()
                    recurrence(l, 1 - b)
                    attention(b)
                    gate_sigmoids(l)
                elif name == "rnn_out":
                    plain(k)
                elif name == "attn_out":
                    attn_out(k, 1 - b)
                elif name == "mix_out":
                    into_x(k, gain_of("ffn2_norm", l), b)
                elif name == "ple":
                    act.wait_ge(q.in_p, 16 * (l + 1))
                    nc.scalar.activation(pthi[:, :, :], ptraw[:, :, :], ACT.Copy).then_inc(q.pt_hi, 1)
                    into_x(k, gain_of("ffn1_norm", l + 1) if l + 1 < L else None, 1 - b,
                           gated=COL["ple_b_gate"] + l * KD)
                    b = 1 - b
                elif name == "attn2_in":
                    norm_rstd()
                    squares_of(x, q.x_ready, xr_n)
                    norm_rstd()
                    act.wait_ge(q.mods_ready, 1)
                    shifted(mod(0, 0), b)
                    act.wait_ge(q.in_ctx, 32)
                    squares_of(inp, None, None)
                    norm_rstd()
                    shifted(MODCOL, 1 - b)
                    segment(tallies, act, k, split, lambda i, s: seen.take(), lead=SLOTS, straight=True)
                    attention2(b)
                elif name == "attn2_out":
                    y_out(k, 1)
                    residual(mod(0, 3), b)
                elif name == "ffn3_in":
                    ffn_conv_in(k, layer2)
                elif name == "ffn3_out":
                    y_out(k, 2)
                    if k + 1 < NSEG:
                        norm_rstd()
                        squares_of(x, q.x_ready, xr_n)
                        norm_rstd()
                        fourier(mod(1, 0), b)
                        layer2 = 1
                    else:
                        norm_rstd()
                elif name == "fourier_out":
                    y_out(k, 1)
                    residual(mod(1, 3), b)

        @block.vector
        def _(dve):
            ahead, seen, silu_free, up_free, hh_n, gate_n, chain = (
                Tally(), Tally(), Tally(-2), Tally(-2), Tally(), Tally(), Tally())
            tallies = [ahead, seen, silu_free, up_free, hh_n, gate_n, chain]

            def split(s, tiles):
                dve.wait_ge(q.hi_done, ahead.take())
                w = slice(0, tiles * P)
                nc.vector.tensor_tensor(wlo[s][:, w], raw[s][:, w], f32(whi[s][:, w]), ALU.subtract).then_inc(q.lo_done, 1)

            def link(ins):
                ins.then_inc(q.dve_chain, 1)
                dve.wait_ge(q.dve_chain, chain.take())

            rms_n = Tally()

            def next_operand(c, gain, buf):
                if gain is not None:
                    dve.wait_ge(q.h_hi, hh_n.take())
                    nc.vector.scalar_tensor_tensor(out=hlo[buf][:, c, :], in0=x[:, c, :], scalar=gain(c),
                                                   in1=f32(hhi[buf][:, c, :]), op0=ALU.mult, op1=ALU.subtract
                                                   ).then_inc(q.rhs_ready, 1)

            def gain_of(name, l):
                return lambda c: cols[:, COL[name] + l * KD + c, :]

            def ffn_in(k):
                def evict(i, s):
                    if isinstance(i, int) and i == 0 and s == 0:
                        dve.wait_ge(q.rms_ready, rms_n.take())
                    j = s // 2
                    dve.wait_ge(q.mm_done, seen.take())
                    if s % 2 == 0:
                        wait(dve, q.silu_done, silu_free.take())
                        nc.vector.tensor_tensor(gr[j][:, :], psum[s][:, 0:S], rstd[:, :], ALU.mult).then_inc(q.evicted, 1)
                    else:
                        wait(dve, q.prod_ready, up_free.take())
                        nc.vector.tensor_tensor(ur[j][:, :], psum[s][:, 0:S], rstd[:, :], ALU.mult).then_inc(q.evicted, 1)

                def weigh(c0, s):
                    acc, u = unit_sums[0][:, :], unit[1 - HBUF[k]][0]
                    if s == 1:
                        wait(dve, q.unit_mm, um_n.take())
                        dve.wait_ge(in_unit[0], unit_n.take(16))
                        link(nc.vector.tensor_scalar(acc, u[:, 0, :], silu_c[:, c0, :], None, ALU.mult))
                    for t in ((), (1,), (2, 3), ())[s]:
                        ins = nc.vector.scalar_tensor_tensor(out=acc, in0=u[:, t, :], scalar=silu_c[:, c0 + t, :], in1=acc,
                                                             op0=ALU.mult, op1=ALU.add)
                        if t < KD // 2 - 1:
                            link(ins)
                        else:
                            ins.then_inc(q.unit_acc, 1)
                segment([t for t in tallies if t is not chain], dve, k, split, evict,
                        units=(weigh, [um_n, unit_n, chain], (1, 16, KD // 2 - 1)))
                f = sum(takes_units(j) for j in range(k))
                dve.wait_ge(q.unit_mm, UNIT_TURNS * (f + 1))
                for to, n, o in ((0, MOD_TURNS, 0), (MODCOL, CTX_TURNS, UNIT_CHUNKS * MOD_TURNS)):
                    a, n = UNIT_CHUNKS * n * f, UNIT_CHUNKS * n
                    bias = COL["mod_b_2"] + a
                    last = nc.vector.tensor_tensor(modv[:, to + a:to + a + n, 0], GEN[0][:, o:o + n],
                                                   cols[:, bias:bias + n, 0], ALU.add)
                last.then_inc(q.mods_in, 1)

            um_n, unit_n = Tally(-1), Tally()

            def ffn_out(k, gain, buf):
                def evict(i, s):
                    if s % 2:
                        c = 2 * i + s // 2
                        dve.wait_ge(q.mm_done, seen.take(2))
                        nc.vector.scalar_tensor_tensor(out=x[:, c, :], in0=psum[s - 1][:, 0:S], scalar=0.5,
                                                       in1=x[:, c, :], op0=ALU.mult, op1=ALU.add).then_inc(q.evicted, 2)
                        next_operand(c, gain, buf)
                segment(tallies, dve, k, split, evict)

            def mix_in(k):
                def evict(i, s):
                    if isinstance(i, int) and i == 0 and s == 0:
                        dve.wait_ge(q.rms_ready, rms_n.take())
                    dve.wait_ge(q.mm_done, seen.take())
                    nc.vector.tensor_tensor(proj[:, SLOTS * i + s, :], psum[s][:, 0:S], rstd[:, :], ALU.mult
                                            ).then_inc(q.evicted, 1)
                segment(tallies, dve, k, split, evict)

            def gated_out(k, gate):
                def evict(i, s):
                    c = SLOTS * i + s
                    dve.wait_ge(q.mm_done, seen.take())
                    nc.vector.tensor_tensor(proj[:, gate + c, :], psum[s][:, 0:S], proj[:, gate + c, :], ALU.mult
                                            ).then_inc(q.evicted, 1)
                segment(tallies, dve, k, split, evict)

            def mix_out(k, gain, buf):
                def evict(i, s):
                    c = SLOTS * i + s
                    dve.wait_ge(q.mm_done, seen.take())
                    nc.vector.tensor_tensor(x[:, c, :], psum[s][:, 0:S], x[:, c, :], ALU.add).then_inc(q.evicted, 1)
                    next_operand(c, gain, buf)
                segment(tallies, dve, k, split, evict)

            def ple(k, gain, buf):
                def evict(i, s):
                    c = SLOTS * i + s
                    if isinstance(i, int) and i == 0 and s == 0:
                        dve.wait_ge(q.rms_ready, rms_n.take())
                    dve.wait_ge(q.mm_done, seen.take())
                    nc.vector.tensor_tensor(gr[s % 2][:, :], psum[s][:, 0:S], rstd[:, :], ALU.mult).then_inc(q.gate_in, 1)
                    dve.wait_ge(q.gate_sig, gate_n.take())
                    link(nc.vector.tensor_tensor(pr[s % 2][:, :], psum[s][:, S:2 * S], sg[s % 2][:, :], ALU.mult))
                    nc.vector.tensor_tensor(x[:, c, :], x[:, c, :], pr[s % 2][:, :], ALU.add).then_inc(q.evicted, 1)
                    next_operand(c, gain, buf)
                segment(tallies, dve, k, split, evict)

            def log1p(u, out, a, z, z2, scale=2.0):
                link(nc.vector.tensor_scalar(a, u, 2.0, None, ALU.add))
                link(nc.vector.reciprocal(z2, a))
                link(nc.vector.tensor_tensor(z, u, z2, ALU.mult))
                link(nc.vector.tensor_tensor(z2, z, z, ALU.mult))
                link(nc.vector.tensor_scalar(a, z2, 1.0 / 17, None, ALU.mult))
                for n in (15, 13, 11, 9, 7, 5, 3):
                    link(nc.vector.scalar_tensor_tensor(out=a, in0=a, scalar=1.0 / n, in1=z2, op0=ALU.add, op1=ALU.mult))
                link(nc.vector.scalar_tensor_tensor(out=a, in0=a, scalar=1.0, in1=z, op0=ALU.add, op1=ALU.mult))
                link(nc.vector.tensor_scalar(out, a, scale, None, ALU.mult))

            fm_n, fe_n = Tally(), Tally()

            def forget_gates(l):
                z, e, m, r, dcum = ft[0][:, :], ft[1][:, :], ft[2][:, :], ft[3][:, :], ft[7][:, :]
                dve.wait_ge(q.f_mm, fm_n.take())
                link(nc.vector.tensor_tensor(z, FB[0:NH, 0:S], rstd[0:NH, :], ALU.mult))
                nc.vector.tensor_scalar(z, z, small[0:NH, FB_COL + l, :], None, ALU.add).then_inc(q.f_z, 1)
                dve.wait_ge(q.f_exp, fe_n.take())
                link(nc.vector.tensor_scalar(m, z, -1.0, 0.0, ALU.mult, ALU.max))
                log1p(e, r, ft[4][:, :], ft[5][:, :], ft[6][:, :])
                link(nc.vector.scalar_tensor_tensor(out=r, in0=m, scalar=-1.0, in1=r, op0=ALU.mult, op1=ALU.subtract))
                link(nc.vector.tensor_tensor_scan(dcum, ones[0:NH, :], r, 0.0, ALU.mult, ALU.add))
                nc.vector.tensor_copy(z, dcum).then_inc(q.dcum_ready, 1)

            c0_n, at_n, mu_n, un_n = Tally(), Tally(), Tally(), Tally()

            def recurrence(l):
                def turn(i):
                    for j in range(2):
                        c = 2 * i + j
                        dve.wait_ge(q.conv_first, c0_n.take())
                        for lag in range(1, CONV):
                            w = cols[:, COL["conv_w"] + (l * CONV + CONV - 1 - lag) * KD + c, :]
                            ins = nc.vector.scalar_tensor_tensor(out=xc[j][:, lag:S], in0=proj[:, RX + c, 0:S - lag],
                                                                 scalar=w, in1=xc[j][:, lag:S], op0=ALU.mult, op1=ALU.add)
                            if lag < CONV - 1:
                                link(ins)
                        ins.then_inc(q.xc_ready, 1)
                    for j in range(2):
                        dve.wait_ge(q.at_done, at_n.take())
                        link(nc.vector.tensor_tensor(mm[j][:, :], ea[j][:, :], ea[j][:, :], ALU.mult))
                        nc.vector.scalar_tensor_tensor(out=mm[j][:, :], in0=mm[j][:, :], scalar=1.0, in1=th[j][:, :],
                                                       op0=ALU.add, op1=ALU.mult).then_inc(q.m_ready, 1)
                    for j in range(2):
                        c = 2 * i + j
                        dve.wait_ge(q.mult_done, mu_n.take())
                        dve.wait_ge(q.u_ready, un_n.take())
                        link(nc.vector.tensor_tensor(mm[j][:, :], mm[j][:, :], u0[j][:, :], ALU.mult))
                        nc.vector.tensor_tensor_scan(proj[:, RX + c, :], ea[j][:, :], mm[j][:, :], 0.0, ALU.mult, ALU.add
                                                     ).then_inc(q.scan_done, 1)
                turns(dve, KD // 2, [c0_n, at_n, mu_n, un_n, chain], turn)

            qr_n, sm_free, sm_n, ex_n, oh_n = Tally(), Tally(-2), Tally(), Tally(), Tally()

            def attention(l, buf):
                def norms(i):
                    for j in range(2):
                        h = 2 * i + j
                        dve.wait_ge(q.qk_rms, qr_n.take())
                        nc.vector.scalar_tensor_tensor(out=proj[:, QC + h, :], in0=proj[:, QC + h, :], scalar=gq[:, l, :],
                                                       in1=rqk[:, j, 0:S], op0=ALU.mult, op1=ALU.mult)
                        nc.vector.scalar_tensor_tensor(out=proj[:, KC + h, :], in0=proj[:, KC + h, :],
                                                       scalar=col("k_norm", l), in1=rqk[:, j, S:2 * S],
                                                       op0=ALU.mult, op1=ALU.mult).then_inc(q.qk_normed, 1)
                turns(dve, NH // 2, [qr_n], norms)

                def heads(i):
                    for j in range(2):
                        h = 2 * i + j
                        wait(dve, q.s_mm, sm_free.take())
                        nc.vector.tensor_scalar(dsel[j][:, :], ft[7][:, :], small[0:NH, ONEHOT_COL + h, :], None, ALU.mult
                                                ).then_inc(q.dsel_ready, 1)
                    for j in range(2):
                        dve.wait_ge(q.s_mm, sm_n.take())
                        for t in range(ST):
                            last = nc.vector.tensor_reduce(stat[j][:, t:t + 1], SC[j][:, t * P:t * P + (t + 1) * P], AX,
                                                           ALU.max, negate=True)
                        last.then_inc(q.max_ready, 1)
                    for j in range(2):
                        dve.wait_ge(q.exp_done, ex_n.take())
                        link(nc.vector.reciprocal(stat[j][:, 4:6], stat[j][:, 2:4]))
                        for t in range(ST):
                            w = slice(t * P, t * P + (t + 1) * P)
                            last = nc.vector.tensor_scalar(pp[j][:, w], pp[j][:, w], stat[j][:, 4 + t:5 + t], None, ALU.mult)
                        last.then_inc(q.p_ready, 1)
                    for j in range(2):
                        h = 2 * i + j
                        dve.wait_ge(q.o_hi, oh_n.take())
                        nc.vector.tensor_tensor(hlo[buf][:, h, :], GEN[j][:, 0:S], f32(hhi[buf][:, h, :]), ALU.subtract
                                                ).then_inc(q.o_ready, 1)
                turns(dve, NH // 2, [sm_free, sm_n, ex_n, oh_n, chain], heads)

            cm_n = Tally()

            def modulation():
                dve.wait_ge(q.mods_in, 2 * L)

                def gains(dst, src, norm, plus):
                    return nc.vector.scalar_tensor_tensor(out=gmod[:, dst:dst + KD, 0], in0=modv[:, src:src + KD, 0], scalar=plus,
                                                          in1=cols[:, COL["norm_g_2"] + norm:COL["norm_g_2"] + norm + KD, 0],
                                                          op0=ALU.add, op1=ALU.mult)
                for l in range(L):
                    for j, (m, plus) in enumerate(((1, 1.0), (2, 0.0), (4, 1.0), (5, 0.0))):
                        gains(gm(l, j), mod(l, m), gm(l, j), plus)
                link(gains(gm(L, 0), MODCOL + KD, gm(0, 0), 1.0))
                dve.drain().then_inc(q.mods_ready, 1)

            def renormed():
                dve.wait_ge(q.rms_ready, rms_n.take())

                def turn(i):
                    for j in range(2):
                        c = 2 * i + j
                        nc.vector.scalar_tensor_tensor(out=x[:, c, :], in0=x[:, c, :], scalar=cols[:, COL["final_norm"] + c, :],
                                                       in1=rstd[:, :], op0=ALU.mult, op1=ALU.mult).then_inc(q.x_ready, 1)
                turns(dve, KD // 2, [], turn)

            def modulated(source, gain, shift, buf):
                dve.wait_ge(q.rms_ready, rms_n.take())

                def turn(i):
                    for j in range(2):
                        c = 2 * i + j
                        wait(dve, q.rhs_ready, hh_n.at(j - 1))
                        nc.vector.scalar_tensor_tensor(out=hn[j][:, :], in0=source[:, c, :], scalar=gmod[:, gain + c, :],
                                                       in1=rstd[:, :], op0=ALU.mult, op1=ALU.mult).then_inc(q.hn_ready, 1)
                    for j in range(2):
                        c = 2 * i + j
                        dve.wait_ge(q.h_hi, hh_n.take())
                        nc.vector.scalar_tensor_tensor(out=hlo[buf][:, c, :], in0=hn[j][:, :], scalar=modv[:, shift + c, :],
                                                       in1=f32(hhi[buf][:, c, :]), op0=ALU.add, op1=ALU.subtract
                                                       ).then_inc(q.rhs_ready, 1)
                turns(dve, KD // 2, [hh_n], turn)

            def residual(gain):
                dve.wait_ge(q.rms_ready, rms_n.take())

                def turn(i):
                    for j in range(2):
                        c = 2 * i + j
                        link(nc.vector.scalar_tensor_tensor(out=pr[j][:, :], in0=y[:, c, :], scalar=gmod[:, gain + c, :],
                                                            in1=rstd[:, :], op0=ALU.mult, op1=ALU.mult))
                        nc.vector.tensor_tensor(x[:, c, :], x[:, c, :], pr[j][:, :], ALU.add).then_inc(q.x_ready, 1)
                turns(dve, KD // 2, [chain], turn)

            def y_out(k, per):
                def evict(i, s):
                    if per == 1 or s % 2:
                        c = SLOTS * i + s if per == 1 else 2 * i + s // 2
                        dve.wait_ge(q.mm_done, seen.take(per))
                        nc.vector.tensor_copy(y[:, c, :], psum[s - (per - 1)][:, 0:S]).then_inc(q.evicted, per)
                segment(tallies, dve, k, split, evict)

            def ffn_conv_in(k, l):
                def evict(i, s):
                    n = SLOTS * i + s
                    seen.take()
                    dve.wait_ge(q.conv_mid, cm_n.take())
                    dst = (gr if s % 2 == 0 else ur)[s // 2]
                    before = cols[:, COL["ffn_conv_w_2"] + 3 * l * 2 * KF + n, :]
                    after = cols[:, COL["ffn_conv_w_2"] + (3 * l + 2) * 2 * KF + n, :]
                    link(nc.vector.scalar_tensor_tensor(out=dst[:, 1:S], in0=psum[s][:, 0:S - 1], scalar=before,
                                                        in1=dst[:, 1:S], op0=ALU.mult, op1=ALU.add))
                    nc.vector.scalar_tensor_tensor(out=dst[:, 0:S - 1], in0=psum[s][:, 1:S], scalar=after,
                                                   in1=dst[:, 0:S - 1], op0=ALU.mult, op1=ALU.add).then_inc(q.evicted, 1)
                segment(tallies + [cm_n], dve, k, split, evict)

            def attn2_in(k):
                def evict(i, s):
                    c = SLOTS * i + s
                    dve.wait_ge(q.mm_done, seen.take())
                    dst, n = (proj[:, c, :], S) if c < KD else (kv2[:, c - KD, :], 2 * S)
                    nc.vector.tensor_copy(dst, psum[s][:, 0:n]).then_inc(q.evicted, 1)
                segment(tallies, dve, k, split, evict, straight=True)

            def attention2(buf):
                for n, (item, gain) in enumerate(NORMED):
                    dve.wait_ge(q.qk_rms, qr_n.take())
                    nc.vector.scalar_tensor_tensor(out=item, in0=item, scalar=col(gain), in1=rqk[:, n % 2, :].rearrange(
                        "p (a s) -> p a s", a=2), op0=ALU.mult, op1=ALU.mult).then_inc(q.qk_normed, 1)
                for n, item in enumerate(ROPED):
                    dve.wait_ge(q.rot_mm, n + 1)
                    if n >= 2:
                        dve.wait_ge(q.roped, n - 1)
                    nc.vector.tensor_tensor(rb[n % 2][:, :], GEN[n % 2][:, 0:S], tab("sin"), ALU.mult).then_inc(q.rope_part, 1)

                def maxima(h):
                    st = stat[h % 2]
                    dve.wait_ge(q.s_mm, sm_n.take())
                    for t in range(ST):
                        last = nc.vector.tensor_reduce(st[:, t:t + 1], psum[2 * (h % 2) + t][:, :], AX, ALU.max)
                    link(last)
                    if h // 2 < NKV2 // 2:
                        nc.vector.tensor_scalar(st[:, 0:2], st[:, 0:2], -SCALE, None, ALU.mult).then_inc(q.max_ready, 1)
                    else:
                        link(nc.vector.tensor_scalar(st[:, 0:2], st[:, 0:2], SCALE, small[:, SINK_COL + h - NH // 2, :],
                                                     ALU.mult, ALU.max))
                        nc.vector.tensor_scalar(st[:, 0:2], st[:, 0:2], -1.0, None, ALU.mult).then_inc(q.max_ready, 1)

                def weights(h):
                    st = stat[h % 2]
                    dve.wait_ge(q.exp_done, ex_n.take())
                    if h // 2 >= NKV2 // 2:
                        link(nc.vector.tensor_tensor(st[:, 2:4], st[:, 2:4], st[:, 6:8], ALU.add))
                    link(nc.vector.reciprocal(st[:, 4:6], st[:, 2:4]))
                    for t in range(ST):
                        last = nc.vector.tensor_scalar(p2[h % 2][:, t, :], p2[h % 2][:, t, :], st[:, 4 + t:5 + t], None, ALU.mult)
                    last.then_inc(q.p_ready, 1)

                def outputs(h):
                    dve.wait_ge(q.pt_mm, L * NH + h + 1)
                    nc.vector.tensor_copy(pt2[h % 2][:, 2:4, :], psum[5][:, :]).then_inc(q.ptd_ready, 1)
                    dve.wait_ge(q.o_hi, oh_n.take())
                    nc.vector.tensor_tensor(hlo[buf][:, h, :], GEN[h % 2][:, 0:S], f32(hhi[buf][:, h, :]), ALU.subtract
                                            ).then_inc(q.o_ready, 1)
                for h in range(NH + 1):
                    if h < NH:
                        maxima(h)
                    if h >= 1:
                        outputs(h - 1)
                    if h < NH:
                        weights(h)

            def fourier(gain, buf):
                dve.wait_ge(q.rms_ready, rms_n.take())
                for c in range(KD):
                    nc.vector.scalar_tensor_tensor(out=hf[:, c, :], in0=x[:, c, :], scalar=gmod[:, gain + c, :], in1=rstd[:, :],
                                                   op0=ALU.mult, op1=ALU.mult).then_inc(q.hf_raw, 1)
                for g in range(NG + 1):
                    if g < NG:
                        dve.wait_ge(q.spec_mm, g + 1)
                        nc.vector.tensor_copy(spec[g % 2][:, 1, :], psum[2 * (g % 2) + 1][:, :]).then_inc(q.spec_ready, 1)
                    for r in range(2 if g >= 1 else 0):
                        c = 2 * (g - 1) + r
                        dve.wait_ge(q.h_hi, hh_n.take())
                        nc.vector.tensor_tensor(hlo[buf][:, c, :], GEN[r][:, 0:S], f32(hhi[buf][:, c, :]), ALU.subtract
                                                ).then_inc(q.rhs_ready, 1)

            dve.wait_ge(q.in_consts, 64)
            dve.wait_ge(q.wf_hi, 1)
            nc.vector.tensor_tensor(wf_lo[:, :], wf_raw[:, :], f32(wf_hi[:, :]), ALU.subtract).then_inc(q.wf_ready, 1)
            nc.vector.tensor_scalar(gq[:, :, 0], cols[:, COL["q_norm"]:COL["q_norm"] + L, 0], SCALE, None, ALU.mult)
            dve.wait_ge(q.lam_exp, 1)
            lam = cols[:, COL["rg_lambda"]:COL["rg_lambda"] + L * KD, 0]
            link(nc.vector.tensor_scalar(lam_t[1][:, :], lam, -1.0, 0.0, ALU.mult, ALU.max))
            log1p(lam_t[0][:, :], lam_t[2][:, :], lam_t[3][:, :], lam_t[4][:, :], lam_t[5][:, :])
            link(nc.vector.tensor_tensor(lam_t[2][:, :], lam_t[2][:, :], lam_t[1][:, :], ALU.add))
            nc.vector.tensor_scalar(neg_sp[:, :, 0], lam_t[2][:, :], -RG_C, None, ALU.mult)
            link(nc.vector.tensor_scalar(pos_sp[:, :, 0], lam_t[2][:, :], RG_C, None, ALU.mult))
            for s in range(LEAD):
                split(s, SEGS[0][2])
            turns(dve, KD // 2, [hh_n], lambda i: [next_operand(2 * i + j, gain_of("ffn1_norm", 0), 0) for j in range(2)])

            b = 0
            layer2 = 0
            for k in range(NSEG):
                name = SEGS[k][0]
                l = k // BLOCK1
                if name in ("ffn1_in", "ffn2_in"):
                    ffn_in(k)
                elif name == "ffn1_out":
                    ffn_out(k, gain_of("mix_norm", l), 1 - b)
                    b = 1 - b
                elif name == "ffn2_out":
                    ffn_out(k, gain_of("ple_norm", l), 1 - b)
                    b = 1 - b
                elif name == "mix_in":
                    mix_in(k)
                    forget_gates(l)
                    recurrence(l)
                    attention(l, b)
                elif name == "rnn_out":
                    dve.wait_ge(q.sig_done, 2 * KD * (l + 1))
                    gated_out(k, GA)
                elif name == "attn_out":
                    gated_out(k, GB)
                elif name == "mix_out":
                    mix_out(k, gain_of("ffn2_norm", l), b)
                elif name == "ple":
                    dve.wait_ge(q.pt_hi, l + 1)
                    nc.vector.tensor_tensor(ptlo[:, :, :], ptraw[:, :, :], f32(pthi[:, :, :]), ALU.subtract
                                            ).then_inc(q.pt_ready, 1)
                    ple(k, gain_of("ffn1_norm", l + 1) if l + 1 < L else None, 1 - b)
                    b = 1 - b
                elif name == "attn2_in":
                    modulation()
                    renormed()
                    modulated(x, gm(0, 0), mod(0, 0), b)
                    modulated(inp, gm(L, 0), MODCOL, 1 - b)
                    attn2_in(k)
                    attention2(b)
                elif name == "attn2_out":
                    y_out(k, 1)
                    residual(gm(0, 1))
                    modulated(x, gm(0, 2), mod(0, 3), b)
                elif name == "ffn3_in":
                    ffn_conv_in(k, layer2)
                elif name == "ffn3_out":
                    y_out(k, 2)
                    residual(gm(layer2, 3))
                    if k + 1 < NSEG:
                        fourier(gm(1, 0), b)
                        layer2 = 1
                elif name == "fourier_out":
                    y_out(k, 1)
                    residual(gm(1, 1))
                    modulated(x, gm(1, 2), mod(1, 3), b)

        @block.gpsimd
        def _(pool):
            seen, silu_n, ah_n, sq_n, add_n, mh_n = Tally(), Tally(2 - 2), Tally(), Tally(), Tally(), Tally()

            def add_square(first, parity):
                pool.wait_ge(q.sq_ready, sq_n.take())
                if first:
                    nc.gpsimd.tensor_copy(ssq[:, :], sq[:, parity, :]).then_inc(q.ssq_add, 1)
                else:
                    pool.wait_ge(q.ssq_add, add_n.at())
                    nc.gpsimd.tensor_tensor(ssq[:, :], ssq[:, :], sq[:, parity, :], ALU.add).then_inc(q.ssq_add, 1)
                add_n.take()

            def is_first(i, j):
                return isinstance(i, int) and i == 0 and j == 0

            def squares(per_turn):
                turns(pool, KD // per_turn, [sq_n, add_n],
                      lambda i: [add_square(is_first(i, j), j % 2) for j in range(per_turn)])

            def ffn_in(k):
                def turn(i, unit_kind=None):
                    for j in range(2):
                        pool.wait_ge(q.silu_done, silu_n.take())
                        pool.wait_ge(q.evicted, seen.take(2))
                        nc.gpsimd.tensor_tensor(pr[j][:, :], sg[j][:, :], ur[j][:, :], ALU.mult).then_inc(q.prod_ready, 1)
                        pool.wait_ge(q.act_hi, ah_n.take())
                        nc.gpsimd.tensor_tensor(actlo[:, 2 * i + j, :], pr[j][:, :], f32(acthi[:, 2 * i + j, :]),
                                                ALU.subtract).then_inc(q.act_ready, 1)
                        if unit_kind is not None and j == 0:
                            unit_rows(unit[1 - HBUF[k]][1])
                if takes_units(k):
                    unit_turns(pool, SEGS[k][1] // SLOTS, [seen, silu_n, ah_n], [us_n, pair_n, um_n], (1, 1, 1), turn)
                else:
                    turns(pool, SEGS[k][1] // SLOTS, [seen, silu_n, ah_n], turn)

            us_n, pair_n, um_n = Tally(), Tally(), Tally(-1)

            def unit_rows(u):
                pool.wait_ge(q.unit_scaled, us_n.take())
                wait(pool, q.unit_mm, um_n.take())
                nc.gpsimd.tensor_tensor(u[:, 0:2, :], u[:, 0:2, :], u[:, 2:4, :], ALU.add).then_inc(q.pool_chain, 1)
                pool.wait_ge(q.pool_chain, pair_n.take())
                nc.gpsimd.tensor_tensor(unit_sums[1][:, :], u[:, 0, :], u[:, 1, :], ALU.add).then_inc(q.unit_sum, 1)

            ws_free, ri_n, u_free, gl_n, gh_n = Tally(-2), Tally(), Tally(-2), Tally(), Tally()

            def recurrence(l, buf):
                pool.wait_ge(q.in_rnn, 64 * (l + 1))
                pool.wait_ge(q.dcum_ready, l + 1)

                def turn(i):
                    for j in range(2):
                        wait(pool, q.gates_mm, ws_free.take())
                        nc.gpsimd.tensor_copy(wst[j][:, :], rnnw[:, 2 * i + j, :, :]).then_inc(q.ws_ready, 1)
                    for j in range(2):
                        pool.wait_ge(q.ri_done, ri_n.take())
                        wait(pool, q.scan_done, u_free.take())
                        nc.gpsimd.tensor_tensor(u0[j][:, :], ri[j][:, 1, :], xc[j][:, :], ALU.mult).then_inc(q.u_ready, 1)
                turns(pool, KD // 2, [ws_free, ri_n, u_free], turn)
                pool.wait_ge(q.scan_done, KD * (l + 1))

                def gelu(i):
                    for j in range(2):
                        c = 2 * i + j
                        pool.wait_ge(q.gelu_done, gl_n.take())
                        nc.gpsimd.tensor_tensor(proj[:, RX + c, :], proj[:, RX + c, :], proj[:, RGATE + c, :], ALU.mult
                                                ).then_inc(q.gated, 1)
                    for j in range(2):
                        c = 2 * i + j
                        pool.wait_ge(q.gated_hi, gh_n.take())
                        nc.gpsimd.tensor_tensor(hlo[buf][:, c, :], proj[:, RX + c, :], f32(hhi[buf][:, c, :]),
                                                ALU.subtract).then_inc(q.gated_ready, 1)
                turns(pool, KD // 2, [gl_n, gh_n], gelu)

            sm_free = Tally(-2)

            def attention(l):
                pool.wait_ge(q.qk_normed, NH * (l + 1))

                def heads(i):
                    for j in range(2):
                        h = 2 * i + j
                        wait(pool, q.s_mm, sm_free.take())
                        nc.gpsimd.tensor_copy(qs[j][:, :], proj[:, QC + h, :])
                        nc.gpsimd.tensor_copy(vs[j][:, :], proj[:, VC + h, :]).then_inc(q.staged, 1)
                turns(pool, NH // 2, [sm_free], heads)

            def rope():
                pool.wait_ge(q.evicted, seen.at())
                pool.wait_ge(q.qk_normed, L * NH + len(NORMED))
                pool.wait_ge(q.in_ctx, 32)
                for n, item in enumerate(ROPED):
                    nc.gpsimd.tensor_tensor(ra[n % 2][:, :], item, tab("cos"), ALU.mult).then_inc(q.pool_chain, 1)
                    pool.wait_ge(q.pool_chain, 2 * L * UNIT_TURNS + n + 1)
                    pool.wait_ge(q.rope_part, n + 1)
                    nc.gpsimd.tensor_tensor(item, ra[n % 2][:, :], rb[n % 2][:, :], ALU.add).then_inc(q.roped, 1)

            def attn_out(buf):
                def turn(i):
                    for s in range(SLOTS):
                        c = SLOTS * i + s
                        pool.wait_ge(q.evicted, seen.take())
                        nc.gpsimd.tensor_tensor(proj[:, GA + c, :], proj[:, GA + c, :], proj[:, GB + c, :], ALU.add
                                                ).then_inc(q.merged, 1)
                        pool.wait_ge(q.merged_hi, mh_n.take())
                        nc.gpsimd.tensor_tensor(hlo[buf][:, c, :], proj[:, GA + c, :], f32(hhi[buf][:, c, :]),
                                                ALU.subtract).then_inc(q.merged_ready, 1)
                turns(pool, KD // SLOTS, [seen, mh_n], turn)

            nc.gpsimd.memset(neg_ones[:, :], -1.0)
            nc.gpsimd.memset(eps_col[:, :], EPS)
            nc.gpsimd.memset(ones[:, :], 1.0).then_inc(q.consts, 1)
            nc.gpsimd.memset(rnnw[:, :, :, :], 0.0).then_inc(q.consts, 1)
            squares(2)
            b = 0
            for k in range(NSEG):
                name = SEGS[k][0]
                l = k // BLOCK1
                if name in ("ffn1_in", "ffn2_in", "ffn3_in"):
                    ffn_in(k)
                elif name in ("ffn1_out", "ffn2_out"):
                    if name == "ffn1_out" and l:
                        nc.gpsimd.memset(rnnw[:, :, :, :], 0.0).then_inc(q.consts, 1)
                    squares(2)
                    seen.take(SEGS[k][1])
                    b = 1 - b
                elif name == "mix_in":
                    seen.take(SEGS[k][1])
                    recurrence(l, 1 - b)
                    attention(l)
                elif name == "rnn_out":
                    seen.take(SEGS[k][1])
                elif name == "attn_out":
                    attn_out(1 - b)
                elif name in ("mix_out", "ple"):
                    squares(4)
                    seen.take(SEGS[k][1])
                    b = 1 - b if name == "ple" else b
                elif name == "attn2_in":
                    squares(2)
                    squares(2)
                    seen.take(SEGS[k][1])
                    rope()
                elif name in ("attn2_out", "fourier_out"):
                    squares(4)
                    squares(2)
                    seen.take(SEGS[k][1])
                elif name == "ffn3_out":
                    squares(2)
                    if k + 1 < NSEG:
                        squares(2)
                    seen.take(SEGS[k][1])



def tables():
    f = np.float32
    t = {"ident": np.eye(P, dtype=f)}
    quarter = HD // 4
    inv = (np.float32(10000.0) ** (-np.arange(quarter, dtype=f) / f(quarter))).astype(f)
    pos = np.arange(S)
    angle = np.stack([(pos // GRID_W).astype(f)[:, None] * inv, (pos % GRID_W).astype(f)[:, None] * inv])
    t["cos"] = np.cos(angle).transpose(0, 2, 1)[:, None].repeat(2, 1).reshape(P, S).astype(f)
    t["sin"] = np.sin(angle).transpose(0, 2, 1)[:, None].repeat(2, 1).reshape(P, S).astype(f)
    swap = np.zeros((P, P), f)
    for a in range(2):
        for i in range(quarter):
            x1, x2 = 2 * a * quarter + i, (2 * a + 1) * quarter + i
            swap[x2, x1], swap[x1, x2] = -1.0, 1.0
    t["swap"] = swap
    t["causal"] = np.where(np.arange(P)[None, :] > np.arange(P)[:, None], f(NEG), f(0))
    key, query = np.arange(S)[None, :], np.arange(S)[:, None]
    window = np.where(np.abs(key - query) > WINDOW, f(NEG), f(0))
    t["window"] = window.reshape(ST, P, S).transpose(1, 0, 2).reshape(P, ST * S)
    tabs, tabs2 = [np.concatenate([t[n] for n in names], axis=1).astype(f) for names in (TABS, TABS2)]
    turn = 2 * np.pi * (np.outer(np.arange(S), np.arange(GD)) % S) / S
    c, s = np.cos(turn) / np.sqrt(S), np.sin(turn) / np.sqrt(S)
    dft = np.stack([np.stack([c, s]), np.stack([c, -s])])
    return tabs, tabs2, np.ascontiguousarray(dft.reshape(2, 2, 2, P, GD).transpose(3, 0, 2, 1, 4)).astype(f)


def layout(a):
    def panels(w, tiles):
        n, k, m = w.shape
        w = w.reshape(n, k // (tiles * P), tiles, P, m // P, P)
        return np.ascontiguousarray(w.transpose(0, 4, 1, 3, 2, 5)).reshape(-1, P, tiles * P)

    def columns(v):
        return np.ascontiguousarray(v).reshape(-1, P).T

    def features(v):
        return np.ascontiguousarray(v.T.reshape(-1, P, v.shape[0]).transpose(1, 0, 2))

    def paired(w):
        n, k, _ = w.shape
        return w.reshape(n, k, 2, KF, P).transpose(0, 1, 3, 2, 4).reshape(n, k, 2 * F)

    w_in = a["w_in"]
    forget = 5 * D
    out = {
        "ffn1_in": panels(paired(a["ffn1_w_in"]), KD), "ffn1_out": panels(a["ffn1_w_out"], KF // 2),
        "mix_in": panels(np.concatenate([w_in[:, :, :forget], w_in[:, :, forget + NH:]], axis=2), KD),
        "rnn_out": panels(a["w_rnn_out"], KD), "attn_out": panels(a["w_attn_out"], KD), "mix_out": panels(a["w_o"], KD),
        "ffn2_in": panels(paired(a["ffn2_w_in"]), KD), "ffn2_out": panels(a["ffn2_w_out"], KF // 2),
        "ple": panels(np.concatenate([a["ple_w_gate"], a["ple_w_proj"]], axis=1), KD + KP),
        "attn2_in": panels(a["attn_w_in_2"], KD), "attn2_out": panels(a["attn_w_out_2"], KD),
        "ffn3_in": panels(paired(a["ffn_w_up_2"]), KD), "ffn3_out": panels(a["ffn_w_down_2"], KF // 2),
        "fourier_out": panels(a["fourier_w_out_2"], KD),
    }
    out["w_f"] = np.ascontiguousarray(w_in[:, :, forget:forget + NH].reshape(L, KD, P, NH).transpose(2, 0, 1, 3)).reshape(P, -1)
    gates = np.stack([a["rg_wa"], a["rg_wx"]], axis=1)
    out["rnn_gates"] = np.ascontiguousarray(gates.reshape(L, 2, KD, 2, RNN_BW, RNN_BW).transpose(0, 1, 3, 4, 2, 5))
    out["mod_w"] = np.ascontiguousarray(
        a["mod_w_2"].reshape(L, 2, KD // 2, P, MODS * D // MOD_UNIT, MOD_UNIT).transpose(0, 4, 1, 3, 2, 5)
    ).reshape(-1, P, KD // 2, MOD_UNIT)
    out["x"] = features(a["x"][0])
    out["ctx"] = features(a["ctx_2"][0])
    out["p"] = np.stack([features(v[0]) for v in a["p"]])

    def pair_columns(v):
        return v.reshape(-1, 2, KF, P).transpose(0, 2, 1, 3)
    vectors = dict(a, ffn_conv_w_2=pair_columns(a["ffn_conv_w_2"]), ffn_conv_b_2=pair_columns(a["ffn_conv_b_2"]))
    out["cols"] = np.concatenate([columns(vectors[n]) for n in COL], axis=1)[:, :, None]
    small = np.zeros((P, 16, 1), np.float32)
    small[0:NH, 0:L, 0] = a["f_b"].T
    small[:, L:L + 4, 0] = a["sink_2"]
    small[0:NH, 8:16, 0] = np.eye(NH, dtype=np.float32)
    out["small"] = small
    out["tabs"], out["tabs2"], out["dft"] = tables()
    return {n: np.ascontiguousarray(v) for n, v in out.items()}


def kernel(**inputs):
    import concourse.bacc as bacc
    from concourse.bass_utils import run_bass_kernel_spmd

    arrays = layout({n: np.asarray(v) for n, v in inputs.items()})
    nc = bacc.Bacc("TRN2", target_bir_lowering=False, num_devices=1)
    d = {n: nc.dram_tensor(f"in_{n}", v.shape, mybir.dt.from_np(v.dtype), kind="ExternalInput").ap()
         for n, v in arrays.items()}
    out = nc.dram_tensor("result", (P, KD, S), F32, kind="ExternalOutput").ap()
    build_program(nc, d, out)
    r = run_bass_kernel_spmd(nc, [{f"in_{n}": v for n, v in arrays.items()}], core_ids=[0])
    y = r.results[0]["result"]
    return np.ascontiguousarray(y.transpose(2, 1, 0)).reshape(1, S, D)
```
